# Optimizing a Trainium2 kernel written in Bass

```python
import functools
import jax, jax.numpy as jnp
from jax import lax
import numpy as np

D_MODEL = 1024
BATCH = 1
SEQ = 128
DEPTH = 2
DEC_BATCH = 1
DEC_SEQ = 512
PAST_LEN = 128

GRID_W = 64
POOL_WIDTH = 256
POOL_GROUPS = 4
POOL_GROUP_DIM = POOL_WIDTH // POOL_GROUPS
POOL_WINDOWS = (2, 4, 8, 16)
NA_HEADS = 8
NA_HEAD_DIM = 64
NA_WIDTH = NA_HEADS * NA_HEAD_DIM
NA_WIN_ROWS = 8
NA_WIN_COLS = 16
GLA_WIDTH = D_MODEL - POOL_WIDTH - NA_WIDTH
GLA_HEADS = 4
GLA_DV = GLA_WIDTH // GLA_HEADS
GLA_DK = GLA_DV // 2
GLA_KEY_WIDTH = GLA_HEADS * GLA_DK
GLA_GATE_RANK = 16
GLA_GATE_TAU = 16.0
GLA_CHUNK = 64
ROPE_THETA = 10000.0
D_FF = -(-8 * D_MODEL // (3 * 256)) * 256
NORM_EPS = 1e-6
IN_SIZES = (POOL_WIDTH, NA_WIDTH, NA_WIDTH, NA_WIDTH, GLA_KEY_WIDTH, GLA_KEY_WIDTH, GLA_WIDTH, GLA_WIDTH, GLA_GATE_RANK, GLA_GATE_RANK)
IN_WIDTH = sum(IN_SIZES)
IN_SPLIT_POINTS = tuple(int(s) for s in np.cumsum(IN_SIZES)[:-1])

kernel_name = 'hybrid_pool_natten_gla_diffusion_step'

def rms_norm(x, gain):
    xf = x.astype(jnp.float32)
    y = xf * lax.rsqrt(jnp.mean(xf * xf, axis=-1, keepdims=True) + NORM_EPS)
    return (y * gain.astype(jnp.float32)).astype(x.dtype)

def axial_rope_tables(L):
    t = jnp.arange(L)
    row = (t // GRID_W).astype(jnp.float32)
    col = (t % GRID_W).astype(jnp.float32)
    half = GLA_DK // 2
    inv_freq = ROPE_THETA ** (-jnp.arange(0, half, 2, dtype=jnp.float32) / half)
    ang_r = (row[:, None] * inv_freq)[:, None, :]
    ang_c = (col[:, None] * inv_freq)[:, None, :]
    return (jnp.cos(ang_r), jnp.sin(ang_r), jnp.cos(ang_c), jnp.sin(ang_c))

def rope_rotate(x, cos, sin):
    n = x.shape[-1] // 2
    x1, x2 = x[..., :n], x[..., n:]
    return jnp.concatenate([x1 * cos - x2 * sin, x2 * cos + x1 * sin], axis=-1)

def apply_axial_rope(x, rope):
    cos_r, sin_r, cos_c, sin_c = rope
    half = x.shape[-1] // 2
    xf = x.astype(jnp.float32)
    out = jnp.concatenate([rope_rotate(xf[..., :half], cos_r, sin_r), rope_rotate(xf[..., half:], cos_c, sin_c)], axis=-1)
    return out.astype(x.dtype)

def pool_mixer(u, w_pool, pool_scale):
    B, L, _ = u.shape
    t = jnp.arange(L)
    uf = u.astype(jnp.float32)
    diffs = []
    for g, win in enumerate(POOL_WINDOWS):
        ug = uf[..., g * POOL_GROUP_DIM:(g + 1) * POOL_GROUP_DIM]
        csum = jnp.concatenate([jnp.zeros((B, 1, POOL_GROUP_DIM), jnp.float32), jnp.cumsum(ug, axis=1)], axis=1)
        lo = jnp.clip(t - win // 2, 0, L)
        hi = jnp.clip(t + win // 2, 0, L)
        mean = (csum[:, hi] - csum[:, lo]) / (hi - lo).astype(jnp.float32)[None, :, None]
        diffs.append(mean - ug)
    d = jnp.stack(diffs, axis=2).astype(u.dtype)
    y = jnp.einsum('blgc,gcd->blgd', d, w_pool).reshape(B, L, POOL_WIDTH)
    return y * pool_scale

def na_context_attn(q, k, v):
    B, L, H, dh = q.shape
    s = jnp.einsum('bqhd,bkhd->bhqk', q, k).astype(jnp.float32) * (dh ** -0.5)
    p = jax.nn.softmax(s, axis=-1).astype(v.dtype)
    return jnp.einsum('bhqk,bkhd->bqhd', p, v).reshape(B, L, H * dh)

def na_latent_attn(q, k, v, k_ctx, v_ctx, rel_bias):
    B, L, H, dh = q.shape
    R = L // GRID_W
    WR = min(NA_WIN_ROWS, R)
    WC = NA_WIN_COLS
    qg = q.reshape(B, R, GRID_W, H, dh)
    kg = k.reshape(B, R, GRID_W, H, dh)
    vg = v.reshape(B, R, GRID_W, H, dh)
    rows = jnp.arange(R)
    cols = jnp.arange(GRID_W)
    row_idx = jnp.clip(rows - WR // 2, 0, R - WR)[:, None] + jnp.arange(WR)
    col_idx = jnp.clip(cols - WC // 2, 0, GRID_W - WC)[:, None] + jnp.arange(WC)
    dr = row_idx - rows[:, None] + (NA_WIN_ROWS - 1)
    dc = col_idx - cols[:, None] + (NA_WIN_COLS - 1)
    bias = rel_bias[:, dr[:, None, :, None], dc[None, :, None, :]]
    bias = jnp.moveaxis(bias, 1, 0).astype(jnp.float32)
    scale = dh ** -0.5
    n_loc = WR * WC

    def row_block(args):
        q_r, ridx, b_r = args
        k_band = jnp.take(kg, ridx, axis=1)
        v_band = jnp.take(vg, ridx, axis=1)
        k_win = k_band[:, :, col_idx]
        v_win = v_band[:, :, col_idx]
        s_loc = jnp.einsum('bwhd,biwjhd->bhwij', q_r, k_win).astype(jnp.float32) * scale + b_r
        s_ctx = jnp.einsum('bwhd,bhnd->bhwn', q_r, k_ctx).astype(jnp.float32) * scale
        s = jnp.concatenate([s_loc.reshape(B, H, GRID_W, n_loc), s_ctx], axis=-1)
        p = jax.nn.softmax(s, axis=-1).astype(v.dtype)
        p_loc = p[..., :n_loc].reshape(B, H, GRID_W, WR, WC)
        p_ctx = p[..., n_loc:]
        return (jnp.einsum('bhwij,biwjhd->bwhd', p_loc, v_win)
                + jnp.einsum('bhwn,bhnd->bwhd', p_ctx, v_ctx))

    o = lax.map(row_block, (jnp.moveaxis(qg, 1, 0), row_idx, bias))
    return jnp.moveaxis(o, 0, 1).reshape(B, L, H * dh)

def gla_chunk_scan(q, k, v, log_a, s0):
    B, L, H, DK = q.shape
    DV = v.shape[-1]
    C = GLA_CHUNK
    N = L // C

    def to_chunks(a):
        return a.astype(jnp.float32).reshape(B, N, C, H, a.shape[-1]).transpose(1, 0, 3, 2, 4)

    mask = jnp.tril(jnp.ones((C, C), dtype=bool))[:, :, None]

    def step(S, inp):
        qc, kc, vc, gc = inp
        b = jnp.cumsum(gc, axis=2)
        o_inter = jnp.einsum('bhtd,bhde->bhte', qc * jnp.exp(b), S)
        decay = jnp.exp(jnp.where(mask, b[:, :, :, None, :] - b[:, :, None, :, :], -jnp.inf))
        attn = jnp.einsum('bhtd,bhsd,bhtsd->bhts', qc, kc, decay)
        o_intra = jnp.einsum('bhts,bhse->bhte', attn, vc)
        b_last = b[:, :, -1:, :]
        S = jnp.exp(b_last[:, :, 0, :])[..., None] * S + jnp.einsum('bhsd,bhse->bhde', kc * jnp.exp(b_last - b), vc)
        return S, o_inter + o_intra

    S, o = lax.scan(step, s0.astype(jnp.float32), (to_chunks(q), to_chunks(k), to_chunks(v), to_chunks(log_a)))
    o = o.transpose(1, 0, 3, 2, 4).reshape(B, L, H, DV)
    return o, S

def gla_mixer(q, k, v, g, lr_f, lr_b, w_gate_f, b_gate_f, w_gate_b, b_gate_b, norm_gain, s0_f, s0_b, rope):
    B, L, _ = q.shape
    q = q.reshape(B, L, GLA_HEADS, GLA_DK) * (GLA_DK ** -0.5)
    k = k.reshape(B, L, GLA_HEADS, GLA_DK)
    v = v.reshape(B, L, GLA_HEADS, GLA_DV)
    if rope is not None:
        q = apply_axial_rope(q, rope)
        k = apply_axial_rope(k, rope)
    la_f = (jax.nn.log_sigmoid((lr_f @ w_gate_f + b_gate_f).astype(jnp.float32)) / GLA_GATE_TAU).reshape(B, L, GLA_HEADS, GLA_DK)
    la_b = (jax.nn.log_sigmoid((lr_b @ w_gate_b + b_gate_b).astype(jnp.float32)) / GLA_GATE_TAU).reshape(B, L, GLA_HEADS, GLA_DK)
    flip = functools.partial(jnp.flip, axis=1)
    o_f, s_f = gla_chunk_scan(q, k, v, la_f, s0_f)
    o_b, s_b = gla_chunk_scan(flip(q), flip(k), flip(v), flip(la_b), s0_b)
    o = rms_norm(o_f + flip(o_b), norm_gain).astype(g.dtype)
    o = o * jax.nn.silu(g.reshape(B, L, GLA_HEADS, GLA_DV))
    return o.reshape(B, L, GLA_WIDTH), s_f, s_b

def swiglu(h, w_ffn_in, w_ffn_out):
    hg, hu = jnp.split(h @ w_ffn_in, 2, axis=-1)
    return (jax.nn.silu(hg) * hu) @ w_ffn_out

def trunk_layer(x, cond, lw, na_fn, s0_f, s0_b, rope):
    B, L, _ = x.shape
    mods = (jax.nn.silu(cond) @ lw['w_ada'] + lw['b_ada'])[:, None, :]
    shift1, scale1, gate1, shift2, scale2, gate2 = jnp.split(mods, 6, axis=-1)
    h = rms_norm(x, lw['norm1_gain']) * (1 + scale1) + shift1
    u_pool, q_na, k_na, v_na, q_la, k_la, v_la, g_la, lr_f, lr_b = jnp.split(h @ lw['w_in'], IN_SPLIT_POINTS, axis=-1)
    y_pool = pool_mixer(u_pool, lw['w_pool'], lw['pool_scale'])
    q_na = rms_norm(q_na.reshape(B, L, NA_HEADS, NA_HEAD_DIM), lw['q_norm_gain'])
    k_na = rms_norm(k_na.reshape(B, L, NA_HEADS, NA_HEAD_DIM), lw['k_norm_gain'])
    v_na = v_na.reshape(B, L, NA_HEADS, NA_HEAD_DIM)
    y_na = na_fn(q_na, k_na, v_na)
    y_la, s_f, s_b = gla_mixer(q_la, k_la, v_la, g_la, lr_f, lr_b, lw['w_gate_f'], lw['b_gate_f'],
                               lw['w_gate_b'], lw['b_gate_b'], lw['gla_norm_gain'], s0_f, s0_b, rope)
    x = x + gate1 * (jnp.concatenate([y_pool, y_na, y_la], axis=-1) @ lw['w_out'])
    h2 = rms_norm(x, lw['norm2_gain']) * (1 + scale2) + shift2
    x = x + gate2 * swiglu(h2, lw['w_ffn_in'], lw['w_ffn_out'])
    return x, k_na.transpose(0, 2, 1, 3), v_na.transpose(0, 2, 1, 3), s_f, s_b

def setup_inputs(seed: int = 0) -> dict:
    key = jax.random.key(seed)
    ks = jax.random.split(key, 26)
    D = D_MODEL

    def nrm(k, shape, s):
        return jax.random.normal(k, shape, jnp.float32) * s

    return {
        'x_prompt': nrm(ks[0], (BATCH, SEQ, D), 1.0),
        'x_sample': nrm(ks[1], (DEC_BATCH, DEC_SEQ, D), 1.0),
        'c': nrm(ks[2], (DEC_BATCH, D), 1.0),
        'cache_na_k': nrm(ks[3], (DEC_BATCH, DEPTH, NA_HEADS, PAST_LEN, NA_HEAD_DIM), 1.0),
        'cache_na_v': nrm(ks[4], (DEC_BATCH, DEPTH, NA_HEADS, PAST_LEN, NA_HEAD_DIM), 1.0),
        'state_gla_fwd': nrm(ks[5], (DEC_BATCH, DEPTH, GLA_HEADS, GLA_DK, GLA_DV), 2.0),
        'state_gla_bwd': nrm(ks[6], (DEC_BATCH, DEPTH, GLA_HEADS, GLA_DK, GLA_DV), 2.0),
        'c_ctx': nrm(ks[7], (D,), 1.0),
        'w_ada': nrm(ks[8], (DEPTH, D, 6 * D), 0.5 * D ** -0.5),
        'b_ada': nrm(ks[9], (DEPTH, 6 * D), 0.02),
        'norm1_gain': 1.0 + nrm(ks[10], (DEPTH, D), 0.02),
        'norm2_gain': 1.0 + nrm(ks[11], (DEPTH, D), 0.02),
        'w_in': nrm(ks[12], (DEPTH, D, IN_WIDTH), D ** -0.5),
        'w_pool': nrm(ks[13], (DEPTH, POOL_GROUPS, POOL_GROUP_DIM, POOL_GROUP_DIM), POOL_GROUP_DIM ** -0.5),
        'pool_scale': 1.0 + nrm(ks[14], (DEPTH, POOL_WIDTH), 0.1),
        'q_norm_gain': 1.0 + nrm(ks[15], (DEPTH, NA_HEAD_DIM), 0.02),
        'k_norm_gain': 1.0 + nrm(ks[16], (DEPTH, NA_HEAD_DIM), 0.02),
        'rel_bias': nrm(ks[17], (DEPTH, NA_HEADS, 2 * NA_WIN_ROWS - 1, 2 * NA_WIN_COLS - 1), 0.5),
        'w_gate_f': nrm(ks[18], (DEPTH, GLA_GATE_RANK, GLA_KEY_WIDTH), GLA_GATE_RANK ** -0.5),
        'b_gate_f': nrm(ks[19], (DEPTH, GLA_KEY_WIDTH), 0.1),
        'w_gate_b': nrm(ks[20], (DEPTH, GLA_GATE_RANK, GLA_KEY_WIDTH), GLA_GATE_RANK ** -0.5),
        'b_gate_b': nrm(ks[21], (DEPTH, GLA_KEY_WIDTH), 0.1),
        'gla_norm_gain': 1.0 + nrm(ks[22], (DEPTH, GLA_DV), 0.02),
        'w_out': nrm(ks[23], (DEPTH, D, D), D ** -0.5),
        'w_ffn_in': nrm(ks[24], (DEPTH, D, 2 * D_FF), D ** -0.5),
        'w_ffn_out': nrm(ks[25], (DEPTH, D_FF, D), D_FF ** -0.5),
    }

def reference(x_prompt, x_sample, c, cache_na_k, cache_na_v, state_gla_fwd, state_gla_bwd, c_ctx,
              w_ada, b_ada, norm1_gain, norm2_gain, w_in, w_pool, pool_scale, q_norm_gain, k_norm_gain,
              rel_bias, w_gate_f, b_gate_f, w_gate_b, b_gate_b, gla_norm_gain, w_out, w_ffn_in, w_ffn_out):
    def layer_weights(l):
        return {'w_ada': w_ada[l], 'b_ada': b_ada[l], 'norm1_gain': norm1_gain[l], 'norm2_gain': norm2_gain[l],
                'w_in': w_in[l], 'w_pool': w_pool[l], 'pool_scale': pool_scale[l],
                'q_norm_gain': q_norm_gain[l], 'k_norm_gain': k_norm_gain[l],
                'w_gate_f': w_gate_f[l], 'b_gate_f': b_gate_f[l], 'w_gate_b': w_gate_b[l], 'b_gate_b': b_gate_b[l],
                'gla_norm_gain': gla_norm_gain[l], 'w_out': w_out[l],
                'w_ffn_in': w_ffn_in[l], 'w_ffn_out': w_ffn_out[l]}

    xp = x_prompt
    zero_state = jnp.zeros((xp.shape[0], GLA_HEADS, GLA_DK, GLA_DV), jnp.float32)
    ks, vs, sfs, sbs = [], [], [], []
    for l in range(DEPTH):
        xp, k_l, v_l, sf_l, sb_l = trunk_layer(xp, c_ctx[None, :], layer_weights(l), na_context_attn,
                                               zero_state, zero_state, None)
        ks.append(k_l)
        vs.append(v_l)
        sfs.append(sf_l)
        sbs.append(sb_l)
    new_na_k = jnp.stack(ks, axis=1)
    new_na_v = jnp.stack(vs, axis=1)
    new_gla_fwd = jnp.stack(sfs, axis=1)
    new_gla_bwd = jnp.stack(sbs, axis=1)

    xs = x_sample
    rope = axial_rope_tables(xs.shape[1])
    for l in range(DEPTH):
        na_fn = functools.partial(na_latent_attn, k_ctx=cache_na_k[:, l], v_ctx=cache_na_v[:, l], rel_bias=rel_bias[l])
        xs = trunk_layer(xs, c, layer_weights(l), na_fn, state_gla_fwd[:, l], state_gla_bwd[:, l], rope)[0]

    return (xp, xs, new_na_k, new_na_v, new_gla_fwd, new_gla_bwd)


_drawn_inputs = setup_inputs


def setup_inputs(seed=0):
    import zlib

    import numpy as np

    out = dict(_drawn_inputs(seed))
    spreads = {}
    factors = {'cache_na_k': 3.261,
     'state_gla_fwd': 7.847,
     'state_gla_bwd': 7.083,
     'norm2_gain': 6.819,
     'pool_scale': 2.968,
     'q_norm_gain': 8.0,
     'k_norm_gain': 2.754,
     'rel_bias': 4.462,
     'gla_norm_gain': 8.0}
    for name, (base, spread) in spreads.items():
        noise = np.random.default_rng([zlib.crc32(name.encode()), seed]).standard_normal(out[name].shape)
        drawn = base * np.exp(spread * noise) if base else spread * noise
        out[name] = __import__('jax').numpy.asarray(drawn.astype(out[name].dtype))
    for name, factor in factors.items():
        out[name] = (out[name] * factor).astype(out[name].dtype)
    return out
```

```python
from contextlib import ExitStack

import concourse.bass as bass
from concourse import mybir

F32 = mybir.dt.float32
F32R = mybir.dt.float32r
ALU = mybir.AluOpType
ACT = mybir.ActivationFunctionType

P = 128
DEPTH = 2
D = 1024
KT = D // P
LAT, CTX = 512, 128
T = LAT + CTX
HALF = T // 2
GW, GR = 64, 8
EPS = 1e-6
PAIRS = 4
FF_CHUNKS = (8, 8, 6)
SUB = 16
CHUNK = 64
NCH = T // CHUNK
NP = T // P
LIMIT = 40.0
TAU = 16.0

T_LR, T_K, T_Q, T_V, T_PAIR = 0, 2, 3, 4, 6
T_G = T_PAIR + 3 * PAIRS
T_POOL = T_G + 2
T_OUT = T_POOL + 2
T_FF = T_OUT + KT
NT = T_FF + sum(2 * n + KT for n in FF_CHUNKS)
WN = NT // 2
NPAR = 9
LRW = 32
NHID = sum(FF_CHUNKS)
NMOD = 48
SHIFT1, SCALE1, GATE1, SHIFT2, SCALE2, GATE2 = range(0, NMOD, KT)
NADA = 8

C_G1, C_G2, C_PS, C_QG, C_KG, C_BF, C_BB, C_LG = 0, 8, 16, 18, 19, 20, 21, 22
NSMALL = 23

V_GROUPS = (0, 16, 8, 24, 40, 32, 48)
BLOCK_GROUPS = ((0, 1), (2, 3), (3, 4), (5, 6))
KEY_START = (0, 8, 24, 32)
BIAS_KIND = (0, 1, 1, 2)

HEAD_STEPS, TAIL_STEPS = 10, 14
GEMM_STEPS = HEAD_STEPS * PAIRS + TAIL_STEPS
STEPS = GEMM_STEPS + 3
MMS = 6 * KT
UNITS = 10
NU = PAIRS * UNITS
CTX_UNIT = 4


def product_at(step):
    if step <= HEAD_STEPS * PAIRS:
        return step * 3 * MMS // HEAD_STEPS
    return min(3 * PAIRS * MMS + (step - HEAD_STEPS * PAIRS) * 4 * MMS // TAIL_STEPS, (3 * PAIRS + 4) * MMS)


def tiles_done(step):
    return [n for n in range(3 * PAIRS + 4) if product_at(step - 1) < (n + 1) * MMS <= product_at(step)] if step else []


def units_at(step, lag):
    n = step - HEAD_STEPS - 1 - lag
    return [(n // UNITS, n % UNITS)] if 0 <= n < NU else []


def gla_scores_at(step):
    return [j for j in range(NP) if step == 4 + j]


def gla_outs_at(step):
    return [j for j in range(NP) if step == 5 + j]


def x_fills_at(step):
    out = [("go", j) for j in gla_outs_at(step)]
    out += [("oT", c, b) for c in range(PAIRS) for b in range(5) if step == 10 * c + 19 + b]
    out += [("vtr", c, i) for c in range(PAIRS) for i in range(2) if step == 10 * c + 10 + i]
    out += [("gsum", i, h) for i in range(2) for h in range(2) if step == 10 * i + 11 + h]
    out += [("qsum", c, h) for c in range(PAIRS) for h in range(2) if step == 10 * c + 4 + h]
    out += [("ksum", c, h) for c in range(PAIRS) for h in range(2) if step == 10 * c + 7 + h]
    out += [("pool", i, h) for i in range(2) for h in range(2) if step == 51 + 3 * i + h]
    return out


FILLS = {
    "S": ["n1", "zf", "rk", "va0", "kdf", "ufa"] + [("sc", j) for j in range(NP)]
    + ["n2"],
    "P": ["n1", "zf", "rk", "va0", "kdp", "ufb", "n2"],
    "O": ["zb", "rq", "va1", "kdb", "uba"] + [("go", j) for j in range(NP)]
    + [("pv", c, u) for c in range(PAIRS) for u in range(UNITS)],
    "X": ["zb", "rq", "va1", "ubb"] + [f for g in range(STEPS) for f in x_fills_at(g)],
}
ROOTS = ["n1", ("q", 0), ("k", 0), ("g", 0), ("q", 1), ("k", 1), ("g", 1), ("q", 2), ("k", 2), ("q", 3), ("k", 3), "n2"]
NR = len(ROOTS)


def before(bank, name, l):
    return l * len(FILLS[bank]) + FILLS[bank].index(name)


def after(bank, name, l):
    return before(bank, name, l) + 1


def norms(l, name):
    return l * (NR - 2) + ROOTS.index(name) - 1


def slot_uses(l, t):
    return l * WN + t // 2


def acc_uses(l, t):
    return l * WN + t // 2 if t % 2 else l * (WN - 1) + (t - 2) // 2


class Count:

    def __init__(self, per_layer):
        self.per_layer, self.n = per_layer, 0

    def up(self, l):
        self.n += 1
        return l * self.per_layer + self.n


DVE_STEPS, ACT_STEPS = 144, 24


def build(nc, a, out):
    ctx = ExitStack()
    with ctx:
        def sb(name, shape, dt=F32, stack=ctx):
            return stack.enter_context(nc.sbuf_tensor(name, shape, dt))

        def sem(name):
            return ctx.enter_context(nc.semaphore(name))

        x = sb("x", [P, KT, T])
        h_hi, h_lo = sb("h_hi", [P, KT, T], F32R), sb("h_lo", [P, KT, T], F32R)
        raw = [sb(f"w_raw{p}", [P, KT * P]) for p in range(2)]
        w_hi = [sb(f"w_hi{p}", [P, KT * P], F32R) for p in range(2)]
        w_lo = [sb(f"w_lo{p}", [P, KT * P], F32R) for p in range(2)]
        mats = sb("mats", [P, 4, P])
        ident, blocks, ones, swap = (mats[:, i, :] for i in range(4))
        rope = sb("rope", [P, 2, T])
        causal = sb("causal", [P, 512])
        heads4 = sb("heads4", [P, 4])
        edges = sb("edges", [P, 2, 2, 2, 8])
        inv_w = sb("inv_w", [P, 2])
        small_all = sb("small_all", [P, DEPTH, NSMALL])
        b_ada = sb("b_ada", [P, DEPTH * NMOD])
        mods_all = sb("mods_all", [P, DEPTH, NMOD, 2])
        small = sb("small", [P, NSMALL])
        mods = sb("mods", [P, NMOD, 2])
        gain = sb("gain", [P, 2, KT, 2])
        state_in = sb("state_in", [P, DEPTH, 2, CHUNK])
        cond = sb("cond", [P, KT, 2])
        wgate = sb("wgate", [LRW, 2 * P])
        wpool = sb("wpool", [P, 2, P])
        PADT = T + 32
        LAT0, CTX0 = 8, LAT + 24
        tmp = sb("tmp", [P, 2, PADT])
        mean = sb("mean", [P, PADT])
        root = sb("root", [P, T])
        with ExitStack() as first:
            lrT = sb("lrT", [LRW, T], F32, first)
        rstd = sb("rstd", [P, T])
        vT = sb("vT", [P, T])
        qn, kn = sb("qn", [P, 2, T]), sb("kn", [P, 2, T])
        bias = [sb(f"bias{e}", [P, 3, 384]) for e in range(2)]
        ctx_k, ctx_v = sb("ctx_k", [P, PAIRS, P]), sb("ctx_v", [P, 512])
        gla_o = sb("gla_o", [P, 2, T])
        row_stat = sb("row_stat", [P, 3, 4])
        decay = sb("decay", [P, 2, NCH])
        final = sb("final", [P, 2, CHUNK])

        with ExitStack() as first:
            ada = [sb(f"w_ada{s}", [P, KT * P], F32, first) for s in range(NADA)]
        with ExitStack() as first:
            kq = sb("kq", [P, 2, T], F32, first)
            kr = sb("kr", [P, T], F32, first)
            qr = sb("qr", [P, T], F32, first)
            z = sb("z", [P, 2, T], F32, first)
            zl = sb("zl", [P, 2, T], F32, first)
            bcum = sb("bcum", [P, 2, T], F32, first)
            kdT = sb("kdT", [P, 2, NP, P], F32, first)
            kk = sb("kk", [P, 2, 2, 2, 4, CHUNK], F32, first)
        y_hi, y_lo = sb("y_hi", [P, KT, T], F32R), sb("y_lo", [P, KT, T], F32R)
        with ExitStack() as first:
            q_heads = sb("q_heads", [P, 2, 4, P], F32, first)
        gate = sb("gate", [P, 2, T])
        with ExitStack() as first:
            s_heads = sb("s_heads", [P, 2, 2, 4 * CHUNK], F32, first)
        v_tok1 = sb("v_tok1", [P, 8, P])
        v_tok = [sb("v_tok0", [P, 8, P]), v_tok1]
        with ExitStack() as first:
            neg_s = sb("neg_s", [P, 384], F32, first)
            prob = sb("prob", [P, 2, 384], F32, first)
            probT = sb("probT", [P, 2, 384], F32, first)
            o_tok = sb("o_tok", [P, NP, P], F32, first)
        v_la = sb("v_la", [P, NP, 256])
        states = sb("states", [P, 2, NCH, CHUNK])
        att = sb("att", [P, 2, 256])

        acc = [ctx.enter_context(nc.psum_tensor(f"acc{p}", [P, 2, 512], F32)) for p in range(2)]
        bank = {n: ctx.enter_context(nc.psum_tensor(f"bank_{n}", [P, 512], F32)) for n in "SPOX"}
        S, PT, O, X = (bank[n] for n in "SPOX")

        x_in, par_in, cond_in, cond_made, layer_in = (sem(n) for n in ("x_in", "par_in", "cond_in", "cond_made", "layer_in"))
        ada_in, ada_used = [sem(f"ada_in{s}") for s in range(NADA)], [sem(f"ada_used{s}") for s in range(NADA)]
        raw_in, hi_made, lo_made, tile_done, acc_free, bias_in, k_out = (
            [sem(f"{n}{p}") for p in range(2)]
            for n in ("raw_in", "hi_made", "lo_made", "tile_done", "acc_free", "bias_in", "k_out"))
        full = {n: sem(f"full_{n}") for n in "SPOX"}
        free = {n: sem(f"free_{n}") for n in "SPOX"}
        pt_full, pt_free = sem("pt_full"), sem("pt_free")
        norm_sq, sq_used = sem("norm_sq"), sem("sq_used")
        gla_sq, root_made, norm_done = sem("gla_sq"), sem("root_made"), sem("norm_done")
        scaled, h_hi_made, h_made = sem("scaled"), sem("h_hi_made"), sem("h_made")
        log_made, args_made, rope_made, exps_made = (sem(n) for n in ("log_made", "args_made", "rope_made", "exps_made"))
        kd_made, qi_made, qe_made = sem("kd_made"), sem("qi_made"), sem("qe_made")
        kk_arg, kk_exp, kk_made = sem("kk_arg"), sem("kk_exp"), sem("kk_made")
        qh_made, sh_made, att_made = sem("qh_made"), sem("sh_made"), sem("att_made")
        scores_made, biased, prob_made = sem("scores_made"), sem("biased"), sem("prob_made")
        pool_d, gate_exp, gated, gated_hi = (sem(n) for n in ("pool_d", "gate_exp", "gated", "gated_hi"))
        hid_hi, hid_lo = sem("hid_hi"), sem("hid_lo")
        dve_step, act_step = sem("dve_step"), sem("act_step")
        ctx_in, v_out, s_out, y_out = sem("ctx_in"), sem("v_out"), sem("s_out"), sem("y_out")

        halves = (slice(0, HALF), slice(HALF, T))

        def two(ap):
            return ap.rearrange("p (h n) -> p h n", h=2)

        def acc_all(p):
            return acc[p][:, :, 0:HALF]

        def grid(ap, col, width):
            return ap[:, 0:LAT].rearrange("p (r w) -> p r w", r=GR)[:, :, col:col + width]

        def by_column(ap):
            lat = ap[:, 0:LAT].rearrange("p (w r) -> p w r", r=GR)
            return lat[:, :, 0:HALF // GW], lat[:, :, HALF // GW:GR], ap[:, LAT:T]

        def acc_parts(p):
            return (acc[p][:, 0, 0:HALF].rearrange("p (r w) -> p w r", w=GW),
                    acc[p][:, 1, 0:LAT - HALF].rearrange("p (r w) -> p w r", w=GW), acc[p][:, 1, LAT - HALF:HALF])

        def wide(ap, n):
            return ap.unsqueeze(2).broadcast_to([P, ap.shape[1], n])

        STREAMS = ((0, slice(0, LAT)), (1, slice(LAT, T)))
        PIECES = ((0, 0, 0, HALF), (0, 1, 0, LAT - HALF), (1, 1, LAT - HALF, HALF))

        def kts_of(t):
            return KT // 2 if t < T_K else KT

        FF_START, t0 = [], T_FF
        for n in FF_CHUNKS:
            FF_START.append(t0)
            t0 += 2 * n + KT

        block = ctx.enter_context(nc.Block())

        @block.sync
        def _(sp):
            sp.dma_start(cond[:], a["cond"]).then_inc(cond_in, 16)
            for s in range(NADA):
                sp.dma_start(ada[s][:], a["w_ada"][s]).then_inc(ada_in[s], 16)
            for n, t in (("b_ada", b_ada), ("small", small_all), ("mats", mats), ("rope", rope), 
                         ("causal", causal), ("heads4", heads4), ("edges", edges), ("inv_w", inv_w),
                         ("state", state_in)):
                sp.dma_start(t[:], a[n]).then_inc(par_in, 16)
            sp.dma_start(x[:], a["x"]).then_inc(x_in, 16)
            with sp.Fori(1, DEPTH * NMOD // NADA) as i:
                for s in range(NADA):
                    sp.wait_ge(ada_used[s], i)
                    sp.dma_start(ada[s][:], a["w_ada"][i * NADA + s]).then_inc(ada_in[s], 16)

            with sp.Fori(0, DEPTH) as l:
                def load(t):
                    sp.wait_ge(lo_made[t % 2], slot_uses(l, t))
                    n = kts_of(t) * P
                    sp.dma_start(raw[t % 2][:, 0:n], a["w"][l * NT + t, :, 0:n]).then_inc(raw_in[t % 2], 16)

                def load_bias(c, e):
                    sp.wait_ge(biased, l * NU + (UNITS * (c - 1) + 5 * (e + 1) if c else 0))
                    sp.dma_start(bias[e][:], a["bias"][l, c, e]).then_inc(bias_in[e], 16)

                sp.wait_ge(free["X"], l * len(FILLS["X"]))
                sp.dma_start(wgate[:], a["wgate"][l]).then_inc(layer_in, 16)
                sp.dma_start(wpool[:], a["wpool"][l]).then_inc(layer_in, 16)
                for t in range(T_OUT):
                    load(t)
                    if t == T_K:
                        sp.wait_ge(free["O"], l * len(FILLS["O"]))
                        sp.dma_start(ctx_k[:], a["ctx_k"][l]).then_inc(ctx_in, 16)
                        sp.dma_start(ctx_v[:], a["ctx_v"][l]).then_inc(ctx_in, 16)
                        load_bias(0, 0)
                        load_bias(0, 1)
                    if t >= T_PAIR + 6 and t % 3 == 2:
                        c = (t - T_PAIR) // 3 - 1
                        if c < PAIRS:
                            load_bias(c, 0)
                            load_bias(c, 1)
                    for c in range(PAIRS):
                        if t == min(T_PAIR + 3 * c + 5, T_OUT - 1):
                            sp.wait_ge(norm_done, norms(l, ("k", c)) + 1)
                            sp.dma_start(out["k"][l, c], kn[:, c % 2, LAT:T]).then_inc(k_out[c % 2], 16)
                            tv = T_PAIR + 3 * c + 2
                            sp.wait_ge(acc_free[tv % 2], acc_uses(l, tv) + 1)
                            sp.dma_start(out["v"][l, c], vT[:, LAT:T]).then_inc(v_out, 16)
                    if t == T_PAIR + 4:
                        sp.wait_ge(free["X"], after("X", "ubb", l))
                        sp.dma_start(out["s"][l], final[:]).then_inc(s_out, 16)

                def load_stage(start, tiles, kts):
                    with sp.Fori(0, tiles // 2) as i:
                        for p in range(2):
                            sp.wait_ge(lo_made[p], slot_uses(l, start) + i)
                            sp.dma_start(raw[p][:, 0:kts * P], a["w"][l * NT + start + 2 * i + p, :, 0:kts * P]
                                         ).then_inc(raw_in[p], 16)

                load_stage(T_OUT, KT, KT)
                for n, start in zip(FF_CHUNKS, FF_START):
                    load_stage(start, 2 * n, KT)
                    load_stage(start + 2 * n, KT, n)

            sp.wait_ge(acc_free[0], DEPTH * (WN - 1))
            sp.wait_ge(acc_free[1], DEPTH * WN)
            sp.dma_start(out["x"], x[:]).then_inc(y_out, 16)
            for s, n in ((k_out[0], 2), (k_out[1], 2), (v_out, 4), (s_out, 1)):
                sp.wait_ge(s, 16 * DEPTH * n)
            sp.wait_ge(y_out, 16)

        @block.gpsimd
        def _(pool):
            pool.wait_ge(par_in, 16 * NPAR)
            with pool.Fori(0, DEPTH) as l:
                def low(p, uses, n):
                    pool.wait_ge(hi_made[p], uses + 1)
                    pool.tensor_tensor(w_lo[p][:, 0:n], raw[p][:, 0:n], w_hi[p][:, 0:n].bitcast(F32),
                                       ALU.subtract).then_inc(lo_made[p], 1)

                def by_head(j):
                    if j == 0:
                        pool.wait_ge(qe_made, l * 2 + 2)
                    else:
                        pool.wait_ge(full["S"], after("S", ("sc", j - 1), l))
                    for d in range(2):
                        pool.tensor_tensor(
                            q_heads[:, d], z[:, d, j * P:(j + 1) * P].unsqueeze(1).broadcast_to([P, 4, P]),
                            wide(heads4[:], P), ALU.mult).then_inc(qh_made, 1)
                    if j == 0:
                        pool.wait_ge(free["S"], after("S", "ufa", l))
                        pool.wait_ge(free["X"], after("X", "ubb", l))
                    else:
                        pool.wait_ge(full["X"], after("X", ("go", j - 1), l))
                    for d in range(2):
                        for ch in range(2):
                            pool.tensor_tensor(
                                s_heads[:, d, ch].rearrange("p (h n) -> p h n", h=4),
                                states[:, d, 2 * j + ch, :].unsqueeze(1).broadcast_to([P, 4, CHUNK]),
                                wide(heads4[:], CHUNK), ALU.mult).then_inc(sh_made, 1)

                for t in range(T_OUT):
                    low(t % 2, slot_uses(l, t), kts_of(t) * P)
                    if t == T_PAIR + 2:
                        for j in range(NP):
                            by_head(j)
                with pool.Fori(0, (NT - T_OUT) // 2) as i:
                    for p in range(2):
                        low(p, slot_uses(l, T_OUT) + i, KT * P)

        @block.scalar
        def _(act):
            act.wait_ge(cond_in, 16)
            act.activation(cond[:], cond[:], ACT.Silu).then_inc(cond_made, 1)
            act.wait_ge(x_in, 16)

            with act.Fori(0, DEPTH) as l:
                steps = Count(ACT_STEPS)

                def link(ins):
                    ins.then_inc(act_step, 1)
                    act.wait_ge(act_step, steps.up(l))

                def high(p, uses, n=KT * P):
                    act.wait_ge(raw_in[p], (uses + 1) * 16)
                    act.wait_ge(tile_done[p], uses)
                    act.activation(w_hi[p][:, 0:n], raw[p][:, 0:n], ACT.Copy).then_inc(hi_made[p], 1)

                def high_tile(t):
                    high(t % 2, slot_uses(l, t), kts_of(t) * P)

                def inverse_root(waits):
                    for s, n in waits:
                        act.wait_ge(s, n)
                    link(act.activation(root[:], mean[:, 0:T], ACT.Ln))
                    act.activation(root[:], root[:], ACT.Exp, scale=-0.5).then_inc(root_made, 1)

                def norm(w):
                    for k in range(KT):
                        if w:
                            act.wait_ge(acc_free[k % 2], acc_uses(l, T_OUT + k) + 1)
                        if k >= 2:
                            act.wait_ge(sq_used, l * 14 + w * 7 + k - 1)
                        act.activation(tmp[:, k % 2, 0:T], x[:, k, :], ACT.Square).then_inc(norm_sq, 1)
                    inverse_root(((free["S"], after("S", ("n1", "n2")[w], l)), (free["P"], after("P", ("n1", "n2")[w], l))))
                    for k in range(KT):
                        act.wait_ge(scaled, l * 16 + w * 8 + k + 1)
                        for s, cols in STREAMS:
                            ins = act.activation(h_hi[:, k, cols], tmp[:, k % 2, cols], ACT.Identity,
                                                 bias=mods[:, (SHIFT1, SHIFT2)[w] + k, s:s + 1])
                        ins.then_inc(h_hi_made, 1)

                def evacuate(t, dst, scale=1.0):
                    act.wait_ge(tile_done[t % 2], slot_uses(l, t) + 1)
                    return act.activation(two(dst), acc_all(t % 2), ACT.Copy, scale=scale)

                def evacuate_by_column(t, dst):
                    act.wait_ge(tile_done[t % 2], slot_uses(l, t) + 1)
                    for to, part in zip(by_column(dst), acc_parts(t % 2)):
                        ins = act.activation(to, part, ACT.Copy)
                    return ins

                high_tile(0)
                high_tile(1)
                act.wait_ge(acc_free[0], l * (WN - 1))
                act.wait_ge(acc_free[1], l * WN)
                norm(0)
                high_tile(T_K)
                high_tile(T_Q)
                evacuate(T_K, kq[:, 0, :]).then_inc(acc_free[T_K % 2], 1)
                high_tile(T_V)
                for d, (b, n) in enumerate((("P", "zf"), ("X", "zb"))):
                    act.wait_ge(free[b], after(b, n, l))
                    link(act.activation(zl[:, d, :], z[:, d, :], ACT.Abs))
                    link(act.activation(zl[:, d, :], zl[:, d, :], ACT.Exp, scale=-1.0))
                    act.activation(zl[:, d, :], zl[:, d, :], ACT.Ln, bias=1.0).then_inc(log_made, 1)
                evacuate(T_Q, kq[:, 1, :], 32 ** -0.5).then_inc(acc_free[T_Q % 2], 1)
                high_tile(T_V + 1)
                act.wait_ge(v_out, 16 * 4 * l)
                evacuate(T_V, vT[:]).then_inc(acc_free[T_V % 2], 1)
                high_tile(T_PAIR)
                for i, buf in enumerate((zl, z)):
                    for d in range(2):
                        act.wait_ge(args_made, l * 2 + d + 1)
                        act.activation(buf[:, d, :], buf[:, d, :], ACT.Exp, scale=1.0 / TAU).then_inc(exps_made, 1)
                for d, end in ((0, CHUNK - 1), (1, 0)):
                    act.activation(decay[:, d, :], bcum[:, d, end:T:CHUNK], ACT.Exp, scale=1.0 / TAU).then_inc(exps_made, 1)
                act.wait_ge(full["P"], after("P", "va0", l))
                evacuate(T_V + 1, vT[:]).then_inc(acc_free[(T_V + 1) % 2], 1)
                high_tile(T_PAIR + 1)
                act.wait_ge(rope_made, l + 1)
                for d in range(2):
                    act.activation(kq[:, d, :], bcum[:, d, :], ACT.Exp, scale=1.0 / TAU).then_inc(exps_made, 1)

                for g in range(STEPS):
                    for j in range(NP):
                        if g == 3 + j:
                            act.wait_ge(kk_arg, l * NP + j + 1)
                            act.activation(kk[:, j % 2], kk[:, j % 2], ACT.Exp, scale=1.0 / TAU).then_inc(kk_exp, 1)
                    for name in x_fills_at(g - 1):
                        if name[0] in ("qsum", "ksum", "gsum") and name[2]:
                            inverse_root(((free["X"], after("X", name, l)),))
                    for n in tiles_done(g):
                        t = T_PAIR + n
                        if t + 2 < T_OUT:
                            high_tile(t + 2)
                        else:
                            high(t % 2, slot_uses(l, t + 2))
                        if n < 3 * PAIRS and n % 3 < 2:
                            c = n // 3
                            if n % 3:
                                act.wait_ge(k_out[c % 2], 16 * (l * 2 + c // 2))
                            row = (qn, kn)[n % 3][:, c % 2, :]
                            link(evacuate_by_column(t, row))
                            act.wait_ge(norm_done, norms(l, ("qk"[n % 3], c)))
                            act.activation(root[:], row, ACT.Square).then_inc(acc_free[t % 2], 1)
                        elif n < 3 * PAIRS:
                            c = n // 3
                            act.wait_ge(v_out, 16 * (l * 4 + c))
                            act.wait_ge(full["X"], after("X", ("vtr", c - 1, 1) if c else "va1", l))
                            evacuate_by_column(t, vT[:]).then_inc(acc_free[t % 2], 1)
                        elif t < T_POOL:
                            i = t - T_G
                            evacuate(t, gate[:, i, :]).then_inc(acc_free[t % 2], 1)
                            act.wait_ge(acc_free[t % 2], acc_uses(l, t) + 1)
                            act.activation(tmp[:, i, 0:T], gate[:, i, :], ACT.Exp, scale=-1.0).then_inc(gate_exp, 1)
                    for i in range(2):
                        if g == 10 * i + 11:
                            act.wait_ge(free["X"], after("X", ("go", NP - 1), l))
                            act.wait_ge(norm_done, norms(l, ("g", i)))
                            act.activation(root[:], gla_o[:, i, :], ACT.Square).then_inc(gla_sq, 1)
                    for c, u in units_at(g, 1):
                        n = l * NU + c * UNITS + u
                        w = 384 if u % 5 < CTX_UNIT else P
                        act.wait_ge(biased, n + 1)
                        act.activation(prob[:, u % 2, 0:w], neg_s[:, 0:w], ACT.Exp, bias=row_stat[:, 0, u % 4:u % 4 + 1],
                                       scale=-1.0, accum_out=row_stat[:, 1, u % 4:u % 4 + 1]).then_inc(prob_made, 1)
                    for c, u in units_at(g, 2):
                        n = l * NU + c * UNITS + u
                        w = 384 if u % 5 < CTX_UNIT else P
                        act.wait_ge(pt_full, n + 1)
                        if c or u >= 2:
                            m = c * UNITS + u - 2
                            act.wait_ge(full["O"], after("O", ("pv", m // UNITS, m % UNITS), l))
                        act.activation(probT[:, u % 2, 0:w], PT[:, 0:w], ACT.Copy).then_inc(pt_free, 1)
                    for i in range(2):
                        if g == 50 + i:
                            act.wait_ge(gated, l * 2 + i + 1)
                            act.activation(y_hi[:, 6 + i, :], gla_o[:, i, :], ACT.Copy).then_inc(gated_hi, 1)

                def high_pairs(start, tiles, last=False):
                    with act.Fori(0, tiles // 2) as i:
                        high(1, slot_uses(l, start) + i)
                        high(0, slot_uses(l, start) + i + 1)

                with act.Fori(0, KT // 2 - 1) as i:
                    for p in range(2):
                        high(p, slot_uses(l, T_OUT) + i + 1)
                high(0, slot_uses(l, T_FF))
                norm(1)
                for chunk, (n, start) in enumerate(zip(FF_CHUNKS, FF_START)):
                    with act.Fori(0, n) as j:
                        high(1, slot_uses(l, start) + j)
                        act.wait_ge(tile_done[0], slot_uses(l, start) + j + 1)
                        act.activation(two(tmp[:, 0, 0:T]), acc_all(0), ACT.Silu).then_inc(acc_free[0], 1)
                        high(0, slot_uses(l, start) + j + 1)
                        act.wait_ge(acc_free[1], acc_uses(l, start + 1) + j + 1)
                        act.activation(y_hi[:, bass.ds(j, 1), :].rearrange("p a n -> p (a n)"), tmp[:, 1, 0:T],
                                       ACT.Copy).then_inc(hid_hi, 1)
                    if chunk < len(FF_CHUNKS) - 1:
                        high_pairs(start + 2 * n, KT)
                    else:
                        with act.Fori(0, KT // 2 - 1) as i:
                            high(1, slot_uses(l, start + 2 * n) + i)
                            high(0, slot_uses(l, start + 2 * n) + i + 1)
                        high(1, slot_uses(l, start + 2 * n) + KT // 2 - 1)
                assert steps.n == ACT_STEPS, steps.n

        @block.vector
        def _(dve):
            dve.memset(mean[:], 0.0).then_inc(dve_step, 1)
            dve.wait_ge(dve_step, 1)
            dve.wait_ge(par_in, 16 * NPAR)
            for s in range(NADA):
                dve.wait_ge(ada_used[s], DEPTH * NMOD // NADA)
            dve.tensor_tensor(mods_all[:].rearrange("p l m s -> p (l m) s"),
                              X[:, 0:DEPTH * NMOD * 2].rearrange("p (m s) -> p m s", s=2), wide(b_ada[:], 2),
                              ALU.add).then_inc(dve_step, 1)
            dve.wait_ge(dve_step, 2)
            dve.wait_ge(x_in, 16)

            with dve.Fori(0, DEPTH) as l:
                steps = Count(DVE_STEPS)

                def link(ins):
                    ins.then_inc(dve_step, 1)
                    dve.wait_ge(dve_step, steps.up(l) + 2)

                def take(b, name):
                    dve.wait_ge(full[b], after(b, name, l))

                def newton(name):
                    dve.wait_ge(root_made, l * NR + ROOTS.index(name) + 1)
                    link(dve.tensor_tensor(rstd[:], root[:], root[:], ALU.mult))
                    link(dve.scalar_tensor_tensor(out=rstd[:], in0=rstd[:], scalar=-0.5, in1=mean[:, 0:T],
                                                  op0=ALU.mult, op1=ALU.mult))
                    return dve.scalar_tensor_tensor(out=rstd[:], in0=rstd[:], scalar=1.5, in1=root[:],
                                                    op0=ALU.add, op1=ALU.mult)

                def mean_from(b, name, half, width):
                    take(b, name)
                    dve.tensor_scalar(mean[:, halves[half]], bank[b][:, 0:HALF], 1.0 / width, EPS,
                                      ALU.mult, ALU.add).then_inc(free[b], 1)

                def norm(w):
                    name = ("n1", "n2")[w]
                    shift = (SHIFT1, SHIFT2)[w]
                    mean_from("S", name, 0, D)
                    mean_from("P", name, 1, D)
                    link(newton(name))

                    def scale(k):
                        for s, cols in STREAMS:
                            ins = dve.scalar_tensor_tensor(out=tmp[:, k % 2, cols], in0=x[:, k, cols],
                                                           scalar=gain[:, w, k, s:s + 1], in1=rstd[:, cols],
                                                           op0=ALU.mult, op1=ALU.mult)
                        ins.then_inc(scaled, 1)

                    scale(0)
                    for k in range(KT):
                        if k + 1 < KT:
                            if k:
                                dve.wait_ge(h_made, l * 16 + w * 8 + k)
                            scale(k + 1)
                        dve.wait_ge(h_hi_made, l * 16 + w * 8 + k + 1)
                        for s, cols in STREAMS:
                            ins = dve.scalar_tensor_tensor(out=h_lo[:, k, cols], in0=tmp[:, k % 2, cols],
                                                           scalar=mods[:, shift + k, s:s + 1],
                                                           in1=h_hi[:, k, cols].bitcast(F32),
                                                           op0=ALU.add, op1=ALU.subtract)
                        ins.then_inc(h_made, 1)

                dve.wait_ge(acc_free[0], l * (WN - 1))
                dve.wait_ge(acc_free[1], l * WN)
                dve.tensor_copy(small[:], small_all[:, bass.ds(l, 1), :].rearrange("p a n -> p (a n)"))
                link(dve.tensor_copy(mods[:], mods_all[:, bass.ds(l, 1), :, :].rearrange("p a m s -> p (a m) s")))
                for w, (sc, g) in enumerate(((SCALE1, C_G1), (SCALE2, C_G2))):
                    dve.scalar_tensor_tensor(out=gain[:, w], in0=mods[:, sc:sc + KT, :], scalar=1.0,
                                             in1=wide(small[:, g:g + KT], 2), op0=ALU.add, op1=ALU.mult)
                link(dve.tensor_scalar(small[:, C_QG:C_QG + 1], small[:, C_QG:C_QG + 1], 64 ** -0.5, None, ALU.mult))

                norm(0)
                dve.wait_ge(tile_done[1], slot_uses(l, 1) + 1)
                dve.tensor_copy(two(lrT[:]), acc[1][0:LRW, :, 0:HALF]).then_inc(acc_free[1], 1)
                for d, (b0, b1, name, col) in enumerate((("S", "P", "zf", C_BF), ("O", "X", "zb", C_BB))):
                    for half, b in enumerate((b0, b1)):
                        take(b, name)
                        dve.tensor_scalar(z[:, d, halves[half]], bank[b][:, 0:HALF], small[:, col:col + 1], None,
                                          ALU.add).then_inc(free[b], 1)

                def rotate(i, t, b0, b1, name, dst):
                    dve.wait_ge(acc_free[t % 2], acc_uses(l, t) + 1)
                    dve.tensor_tensor(tmp[:, 0, 0:T], kq[:, i, :], rope[:, 0, :], ALU.mult)
                    for half, b in enumerate((b0, b1)):
                        take(b, name)
                        dve.tensor_tensor(tmp[:, 1, halves[half]], bank[b][:, 0:HALF], rope[:, 1, halves[half]],
                                          ALU.mult).then_inc(free[b], 1)
                    dve.wait_ge(free[b1], after(b1, name, l))
                    return dve.tensor_tensor(dst[:], tmp[:, 0, 0:T], tmp[:, 1, 0:T], ALU.add)

                link(rotate(0, T_K, "S", "P", "rk", kr))
                link(dve.memset(root[:], 1.0))
                link(dve.memset(root[:, 0:T:CHUNK], 0.0))
                for d in range(2):
                    dve.wait_ge(log_made, l * 2 + d + 1)
                    link(dve.scalar_tensor_tensor(out=z[:, d, :], in0=z[:, d, :], scalar=0.0, in1=zl[:, d, :],
                                                  op0=ALU.min, op1=ALU.subtract))
                    turn = slice(None, None, -1) if d else slice(None)
                    link(dve.tensor_tensor_scan(bcum[:, d, turn], root[:], z[:, d, turn], 0.0, ALU.mult, ALU.add))
                for b, n, cols in (("S", 4, slice(0, 4)), ("P", 1, slice(4, 5))):
                    take(b, "va0")
                    dve.tensor_copy(v_la[:, cols, 0:P], bank[b][:, 0:n * P].rearrange("p (n f) -> p n f", f=P)
                                    ).then_inc(free[b], 1)
                for d in range(2):
                    end = (CHUNK - 1, 0)[d]
                    sub = bcum[:, d, :].rearrange("p (n s) -> p n s", s=SUB)
                    whole = bcum[:, d, :].rearrange("p (n s) -> p n s", s=CHUNK)
                    link(dve.tensor_tensor(z[:, d, :].rearrange("p (n s) -> p n s", s=SUB), sub,
                                           wide(bcum[:, d, SUB // 2:T:SUB], SUB), ALU.subtract))
                    dve.tensor_scalar(z[:, d, :], z[:, d, :], LIMIT * TAU, None, ALU.min)
                    dve.tensor_tensor(zl[:, d, :].rearrange("p (n s) -> p n s", s=CHUNK),
                                      wide(bcum[:, d, end:T:CHUNK], CHUNK), whole, ALU.subtract).then_inc(args_made, 1)
                rotate(1, T_Q, "O", "X", "rq", qr).then_inc(rope_made, 1)
                dve.wait_ge(rope_made, l + 1)
                for b, n, cols in (("O", 4, slice(0, 4)), ("X", 1, slice(4, 5))):
                    take(b, "va1")
                    dve.tensor_copy(v_la[:, cols, P:2 * P], bank[b][:, 0:n * P].rearrange("p (n f) -> p n f", f=P)
                                    ).then_inc(free[b], 1)
                for i, (buf, fac, made) in enumerate(((zl, kr, kd_made), (z, qr, qe_made), (None, None, None), (kq, qr, qi_made))):
                    for d in range(2):
                        if buf is None:
                            continue
                        dve.wait_ge(exps_made, l * 8 + 2 * i + d + 1)
                        dve.tensor_tensor(buf[:, d, :], buf[:, d, :], fac[:], ALU.mult).then_inc(made, 1)
                take("S", "kdf")
                dve.tensor_copy(kdT[:, 0, 0:4, :], S[:].rearrange("p (n f) -> p n f", f=P)).then_inc(free["S"], 1)
                take("P", "kdp")
                dve.tensor_copy(kdT[:, :, 4, :], PT[:, 0:2 * P].rearrange("p (d f) -> p d f", f=P)).then_inc(free["P"], 1)
                take("O", "kdb")
                dve.tensor_copy(kdT[:, 1, 0:4, :], O[:].rearrange("p (n f) -> p n f", f=P)).then_inc(free["O"], 1)
                dve.tensor_copy(states[:, 0, 0, :], state_in[:, bass.ds(l, 1), 0, :].rearrange("p a n -> p (a n)"))
                dve.tensor_copy(states[:, 1, 7, :], state_in[:, bass.ds(l, 1), 1, :].rearrange("p a n -> p (a n)"))
                dve.memset(states[:, 0, 8, :], 0.0)
                dve.memset(states[:, 1, 9, :], 0.0)
                for b, name in (("S", "ufa"), ("P", "ufb"), ("O", "uba"), ("X", "ubb")):
                    take(b, name)

                def added(d, n):
                    return (("S", "P"), ("O", "X"))[d][n % 2], slice(n // 2 * CHUNK, n // 2 * CHUNK + CHUNK)

                def scan(d, n, dst):
                    b, cols = added(d, n)
                    return dve.scalar_tensor_tensor(out=dst, in0=states[:, d, n, :], scalar=decay[:, d, n:n + 1],
                                                    in1=bank[b][:, cols], op0=ALU.mult, op1=ALU.add)

                dve.wait_ge(s_out, 16 * l)
                for d, n in ((0, 8), (1, 9)):
                    b, cols = added(d, n)
                    link(dve.tensor_copy(states[:, d, 17 - n, :], bank[b][:, cols]))
                scan(0, 9, final[:, 0, :])
                scan(1, 8, final[:, 1, :])
                for i in range(7):
                    f = scan(0, i, states[:, 0, i + 1, :])
                    if i < 5:
                        f.then_inc(dve_step, 1)
                        nf = steps.up(l) + 2
                    else:
                        f.then_inc(free["PS"[i - 5]], 1)
                    r = scan(1, 7 - i, states[:, 1, 6 - i, :])
                    if i < 5:
                        r.then_inc(dve_step, 1)
                        nf = steps.up(l) + 2
                        dve.wait_ge(dve_step, nf)
                    else:
                        r.then_inc(free["OX"[i - 5]], 1)
                        dve.wait_ge(free["PS"[i - 5]], after("PS"[i - 5], ("ufb", "ufa")[i - 5], l))
                        dve.wait_ge(free["OX"[i - 5]], after("OX"[i - 5], ("uba", "ubb")[i - 5], l))

                def kk_args(j):
                    for d in range(2):
                        b = bcum[:, d, j * P:(j + 1) * P]
                        ref = b[:, SUB // 2:P:SUB].rearrange("p (c i) -> p c i", c=2)
                        for ch in range(2):
                            ins = dve.tensor_tensor(
                                kk[:, j % 2, d, ch], wide(ref[:, ch, :], CHUNK),
                                b[:, ch * CHUNK:(ch + 1) * CHUNK].unsqueeze(1).broadcast_to([P, 4, CHUNK]), ALU.subtract)
                    link(ins)
                    dve.tensor_scalar(kk[:, j % 2], kk[:, j % 2], LIMIT * TAU, None, ALU.min).then_inc(kk_arg, 1)

                def kk_mul(j):
                    dve.wait_ge(kk_exp, l * NP + j + 1)
                    kj = kr[:, j * P:(j + 1) * P]
                    for d in range(2):
                        for ch in range(2):
                            ins = dve.tensor_tensor(
                                kk[:, j % 2, d, ch], kk[:, j % 2, d, ch],
                                kj[:, ch * CHUNK:(ch + 1) * CHUNK].unsqueeze(1).broadcast_to([P, 4, CHUNK]), ALU.mult)
                    ins.then_inc(kk_made, 1)

                def gla_mask(j):
                    take("S", ("sc", j))
                    dve.tensor_tensor(tmp[:, j % 2, 0:512], S[:], causal[:], ALU.mult).then_inc(free["S"], 1)
                    dve.wait_ge(free["S"], after("S", ("sc", j), l))
                    dve.tensor_tensor(att[:, j % 2, :], tmp[:, j % 2, 0:256], tmp[:, j % 2, 256:512],
                                      ALU.add).then_inc(att_made, 1)

                def gla_take(j):
                    for ch, b in enumerate("OX"):
                        take(b, ("go", j))
                        dve.tensor_copy(gla_o[:, :, j * P + ch * CHUNK:j * P + (ch + 1) * CHUNK],
                                        bank[b][:, 0:P].rearrange("p (h n) -> p h n", h=2)).then_inc(free[b], 1)

                def square_mean(name):
                    mean_from("X", name, name[2], CHUNK)

                def finish_norm(kind, c):
                    link(newton((kind, c)))
                    dst, col = {"q": (qn, C_QG), "k": (kn, C_KG), "g": (gla_o, C_LG)}[kind]
                    row = dst[:, c if kind == "g" else c % 2, :]
                    dve.scalar_tensor_tensor(out=row, in0=row, scalar=small[:, col:col + 1], in1=rstd[:],
                                             op0=ALU.mult, op1=ALU.mult).then_inc(norm_done, 1)

                def to_pool(i):
                    t = T_POOL + i
                    dve.wait_ge(tile_done[t % 2], slot_uses(l, t) + 1)
                    u, s0, s1 = mean, tmp[:, 0, :], tmp[:, 1, :]
                    dve.memset(mean[:, 0:LAT0], 0.0)
                    dve.memset(mean[:, LAT0 + LAT:CTX0], 0.0)
                    dve.memset(mean[:, CTX0 + CTX:PADT], 0.0)
                    dve.tensor_copy(mean[:, LAT0:LAT0 + HALF], acc[t % 2][:, 0, 0:HALF])
                    dve.tensor_copy(mean[:, LAT0 + HALF:LAT0 + LAT], acc[t % 2][:, 1, 0:LAT - HALF])
                    dve.tensor_copy(mean[:, CTX0:CTX0 + CTX], acc[t % 2][:, 1, LAT - HALF:HALF]).then_inc(acc_free[t % 2], 1)
                    dve.wait_ge(acc_free[t % 2], acc_uses(l, t) + 1)
                    src, reach = mean[:], 1
                    link(dve.tensor_tensor(s0[:, 1:PADT], mean[:, 0:PADT - 1], mean[:, 1:PADT], ALU.add))
                    bufs, lo = (s0, s1), 1
                    for k in range(1, 2 + 2 * i):
                        a_, b_ = bufs[(k - 1) % 2], bufs[k % 2]
                        r = 2 ** (k - 1)
                        n0, n1 = lo + r, PADT - lo - r + 1
                        n1 = PADT - (2 ** k - 1)
                        link(dve.tensor_tensor(b_[:, n0:n1], a_[:, n0 - r:n1 - r], a_[:, n0 + r:n1 + r], ALU.add))
                        lo = n0
                    for rows, src in ((slice(0, 64), s0), (slice(64, P), s1)):
                        for s, (first, last) in enumerate(((LAT0, LAT0 + LAT - 8), (CTX0, CTX0 + CTX - 8))):
                            for e, at in enumerate((first, last)):
                                ins = dve.tensor_tensor(src[rows, at:at + 8], src[rows, at:at + 8],
                                                        edges[rows, i, s, e, :], ALU.mult)
                    link(ins)
                    for rows, src in ((slice(0, 64), s0), (slice(64, P), s1)):
                        for first, cols in ((LAT0, slice(0, LAT)), (CTX0, slice(LAT, T))):
                            n = cols.stop - cols.start
                            ins = dve.scalar_tensor_tensor(out=root[rows, cols], in0=src[rows, first:first + n],
                                                           scalar=inv_w[rows, i:i + 1], in1=mean[rows, first:first + n],
                                                           op0=ALU.mult, op1=ALU.subtract)
                    ins.then_inc(pool_d, 1)

                kk_args(0)
                for g in range(STEPS + 1):
                    for name in x_fills_at(g - 2):
                        if name[0] in ("qsum", "ksum", "gsum") and name[2]:
                            finish_norm(name[0][0], name[1])
                    for j in range(NP):
                        if g == 4 + j:
                            kk_mul(j)
                    for j in range(NP):
                        if g == 5 + j:
                            gla_mask(j)
                        if g == 6 + j:
                            gla_take(j)
                        if j and g == 3 + j:
                            pass
                    for j in range(1, NP):
                        if g == 3 + j:
                            kk_args(j)
                    for c, u in units_at(g, 1):
                        dve.wait_ge(scores_made, l * NU + c * UNITS + u + 1)
                        e, b = u // 5, u % 5
                        w = 384 if b < CTX_UNIT else P
                        if b == 0:
                            dve.wait_ge(bias_in[e], 16 * (l * PAIRS + c + 1))
                        dve.wait_ge(prob_made, l * NU + c * UNITS + u)
                        added_ = bias[e][:, BIAS_KIND[b], :] if b < CTX_UNIT else bias[e][:, 0, 256:384]
                        if units_at(g, 3):
                            (_, v), = units_at(g, 3)
                            dve.reciprocal(row_stat[:, 2, v % 4:v % 4 + 1], row_stat[:, 1, v % 4:v % 4 + 1]
                                           ).then_inc(dve_step, 1)
                            reciprocal_made = steps.up(l) + 2
                        else:
                            dve.memset(row_stat[:, 2, 2 + u % 2:3 + u % 2], 0.0)
                        dve.tensor_tensor_reduce(neg_s[:, 0:w], S[:, 0:w], added_, -1.0, 3e38, ALU.add, ALU.min,
                                                 row_stat[:, 0, u % 4:u % 4 + 1]).then_inc(biased, 1)
                    for c, u in units_at(g, 3):
                        e, b = u // 5, u % 5
                        if units_at(g, 1):
                            dve.wait_ge(dve_step, reciprocal_made)
                        else:
                            dve.wait_ge(prob_made, l * NU + c * UNITS + u + 1)
                            link(dve.reciprocal(row_stat[:, 2, u % 4:u % 4 + 1], row_stat[:, 1, u % 4:u % 4 + 1]))
                        take("O", ("pv", c, u))
                        dve.tensor_scalar(o_tok[:, b, 64 * e:64 * e + 64], O[:, 0:64], row_stat[:, 2, u % 4:u % 4 + 1],
                                          None, ALU.mult).then_inc(free["O"], 1)
                    for name in x_fills_at(g - 1):
                        if name[0] in ("qsum", "ksum", "gsum"):
                            square_mean(name)
                        if name[0] == "vtr":
                            take("X", name)
                            c, i = name[1:]
                            dve.tensor_copy(v_tok[c % 2][:, 4 * i:4 * i + 4, :], X[:].rearrange("p (n f) -> p n f", f=P)
                                            ).then_inc(free["X"], 1)
                        if name[0] == "oT":
                            take("X", name)
                            c, b = name[1:]
                            if b < CTX_UNIT:
                                hi_, lo_ = grid(y_hi[:, 2 + c, :], 16 * b, 16), grid(y_lo[:, 2 + c, :], 16 * b, 16)
                                src = X[:, 0:P].rearrange("p (w r) -> p r w", r=GR)
                            else:
                                hi_, lo_, src = y_hi[:, 2 + c, LAT:T], y_lo[:, 2 + c, LAT:T], X[:, 0:P]
                            link(dve.tensor_copy(hi_, src))
                            dve.tensor_tensor(lo_, src, hi_.bitcast(F32), ALU.subtract).then_inc(free["X"], 1)
                        if name[0] == "pool":
                            take("X", name)
                            i, half = name[1:]
                            hi_, lo_ = y_hi[:, i, halves[half]], y_lo[:, i, halves[half]]
                            link(dve.tensor_scalar(hi_, X[:, 0:HALF], small[:, C_PS + i:C_PS + i + 1], None, ALU.mult))
                            dve.scalar_tensor_tensor(out=lo_, in0=X[:, 0:HALF], scalar=small[:, C_PS + i:C_PS + i + 1],
                                                     in1=hi_.bitcast(F32), op0=ALU.mult, op1=ALU.subtract
                                                     ).then_inc(free["X"], 1)
                    for i in range(2):
                        if g == 45 + 3 * i:
                            dve.wait_ge(gate_exp, l * 2 + i + 1)
                            link(dve.tensor_scalar(tmp[:, i, 0:T], tmp[:, i, 0:T], 1.0, None, ALU.add))
                            link(dve.reciprocal(tmp[:, i, 0:T], tmp[:, i, 0:T]))
                            link(dve.tensor_tensor(gate[:, i, :], gate[:, i, :], tmp[:, i, 0:T], ALU.mult))
                            dve.tensor_tensor(gla_o[:, i, :], gla_o[:, i, :], gate[:, i, :], ALU.mult).then_inc(gated, 1)
                    for i in range(2):
                        if g == 51 + i:
                            dve.wait_ge(gated_hi, l * 2 + i + 1)
                            link(dve.tensor_tensor(y_lo[:, 6 + i, :], gla_o[:, i, :], y_hi[:, 6 + i, :].bitcast(F32),
                                                   ALU.subtract))
                    for i in range(2):
                        if g == 51 + 3 * i:
                            to_pool(i)

                def update(p, m, gates, done, in_loop=True):
                    dve.wait_ge(tile_done[p], done)
                    for n, (s, half, first, last) in enumerate(PIECES):
                        xs = x[:, bass.ds(m, 1), half * HALF + first:half * HALF + last].rearrange("p a n -> p (a n)")
                        ins = dve.scalar_tensor_tensor(
                            out=xs, in0=acc[p][:, half, first:last],
                            scalar=mods[:, bass.ds(gates + m, 1), s:s + 1].rearrange("p a s -> p (a s)"), in1=xs,
                            op0=ALU.mult, op1=ALU.add)
                    ins.then_inc(acc_free[p], 1)

                def updates(start, gates):
                    with dve.Fori(0, KT // 2) as i:
                        for p in range(2):
                            dve.wait_ge(acc_free[p], acc_uses(l, start + p) + i)
                            update(p, 2 * i + p, gates, slot_uses(l, start) + i + 1)

                updates(T_OUT, GATE1)
                norm(1)
                made = 0
                for n, start in zip(FF_CHUNKS, FF_START):
                    with dve.Fori(0, n) as j:
                        dve.wait_ge(tile_done[1], slot_uses(l, start) + j + 1)
                        dve.wait_ge(acc_free[0], acc_uses(l, start) + j + 1)
                        dve.wait_ge(hid_lo, l * NHID + made + j)
                        dve.tensor_tensor(two(tmp[:, 1, 0:T]), two(tmp[:, 0, 0:T]), acc_all(1), ALU.mult
                                          ).then_inc(acc_free[1], 1)
                        dve.wait_ge(hid_hi, l * NHID + made + j + 1)
                        dve.tensor_tensor(y_lo[:, bass.ds(j, 1), :].rearrange("p a n -> p (a n)"), tmp[:, 1, 0:T],
                                          y_hi[:, bass.ds(j, 1), :].rearrange("p a n -> p (a n)").bitcast(F32),
                                          ALU.subtract).then_inc(hid_lo, 1)
                    made += n
                    updates(start + 2 * n, GATE2)
                assert steps.n == DVE_STEPS, steps.n

        @block.tensor
        def _(pe):
            pe.wait_ge(cond_made, 1)
            with pe.Fori(0, DEPTH * NMOD // NADA) as i:
                for s in range(NADA):
                    pe.wait_ge(ada_in[s], (i + 1) * 16)
                    for k in range(KT):
                        mm = pe.matmul(X[:, bass.ds((i * NADA + s) * 2, 2)], ada[s][:, k * P:(k + 1) * P], cond[:, k, :],
                                       start=k == 0, stop=k == KT - 1)
                    mm.then_inc(ada_used[s], 1)
            pe.wait_ge(par_in, 16 * NPAR)

            with pe.Fori(0, DEPTH) as l:
                def claim(b, name):
                    pe.wait_ge(free[b], before(b, name, l))

                def gemm(p, hi, lo, first=0, last=MMS, kts=KT, slot=None, wait_h=False, start=True, stop=True):
                    slot = p if slot is None else slot
                    for n in range(first, min(last, 6 * kts)):
                        k, j = divmod(n, 6)
                        if wait_h and j == 0:
                            pe.wait_ge(h_made, wait_h(k))
                        w = (w_hi, w_hi, w_lo)[j // 2][p]
                        m = (hi, lo, hi)[j // 2]
                        mm = pe.matmul(acc[slot][:, j % 2, 0:HALF], w[:, k % KT * P:(k % KT + 1) * P] if kts <= KT else None,
                                       m(k, j % 2), start=start and n < 2, stop=stop and n >= 6 * kts - 2)
                        if n == 6 * kts - 1:
                            mm.then_inc(tile_done[p], 1)

                def h(part, base=0):
                    return lambda k, half: part[:, base + k, halves[half]]

                def ready(t):
                    pe.wait_ge(lo_made[t % 2], slot_uses(l, t) + 1)
                    pe.wait_ge(acc_free[t % 2], acc_uses(l, t))

                def norm(w):
                    name = ("n1", "n2")[w]
                    claim("S", name)
                    claim("P", name)
                    if w:
                        pe.wait_ge(pt_free, (l + 1) * NU)
                        pe.wait_ge(biased, (l + 1) * NU)
                    for k in range(KT):
                        pe.wait_ge(norm_sq, l * 16 + w * 8 + k + 1)
                        for half, b in enumerate("SP"):
                            mm = pe.matmul(bank[b][:, 0:HALF], ones, tmp[:, k % 2, halves[half]], start=k == 0, stop=k == KT - 1)
                            if k == KT - 1:
                                mm.then_inc(full[b], 1)
                        if k < KT - 1:
                            mm.then_inc(sq_used, 1)

                def both_halves(b0, b1, name, lhsT, row):
                    for half, b in enumerate((b0, b1)):
                        claim(b, name)
                        pe.matmul(bank[b][:, 0:HALF], lhsT, row[:, halves[half]], start=True, stop=True).then_inc(full[b], 1)

                def transposes(b, name, tiles):
                    claim(b, name)
                    for n, src in enumerate(tiles):
                        mm = pe.transpose(bank[b][:, n * P:(n + 1) * P], src, ident)
                    mm.then_inc(full[b], 1)

                norm(0)
                pe.wait_ge(lo_made[0], slot_uses(l, 0) + 1)
                pe.wait_ge(acc_free[1], acc_uses(l, 1))
                gemm(0, h(h_hi), h(h_lo), kts=KT // 2, slot=1, wait_h=lambda k: l * 16 + k + 1, stop=False)
                pe.wait_ge(lo_made[1], slot_uses(l, 1) + 1)
                gemm(1, h(h_hi, KT // 2), h(h_lo, KT // 2), kts=KT // 2, wait_h=lambda k: l * 16 + k + 5, start=False)
                ready(T_K)
                gemm(0, h(h_hi), h(h_lo))
                pe.wait_ge(layer_in, (l + 1) * 32)
                pe.wait_ge(acc_free[1], acc_uses(l, 1) + 1)
                both_halves("S", "P", "zf", wgate[:, 0:P], lrT)
                both_halves("O", "X", "zb", wgate[:, P:2 * P], lrT)
                ready(T_Q)
                gemm(1, h(h_hi), h(h_lo))
                pe.wait_ge(acc_free[T_K % 2], acc_uses(l, T_K) + 1)
                both_halves("S", "P", "rk", swap, kq[:, 0, :])
                ready(T_V)
                gemm(0, h(h_hi), h(h_lo))
                pe.wait_ge(acc_free[T_Q % 2], acc_uses(l, T_Q) + 1)
                both_halves("O", "X", "rq", swap, kq[:, 1, :])
                pe.wait_ge(acc_free[T_V % 2], acc_uses(l, T_V) + 1)
                transposes("S", "va0", [vT[:, n * P:(n + 1) * P] for n in range(4)])
                transposes("P", "va0", [vT[:, 4 * P:5 * P]])
                ready(T_V + 1)
                gemm(1, h(h_hi), h(h_lo))

                def scores(c, u):
                    e, b = u // 5, u % 5
                    rows = slice(64 * e, 64 * e + 64)
                    if u == 0:
                        pe.wait_ge(norm_done, norms(l, ("k", c)) + 1)
                        pe.wait_ge(ctx_in, (l + 1) * 32)
                    if c == u == 0:
                        claim("S", "n2")
                    pe.wait_ge(biased, l * NU + c * UNITS + u)
                    if b < CTX_UNIT:
                        q = qn[rows, c % 2, b * P:(b + 1) * P]
                        k0 = KEY_START[b] * GR
                        pe.matmul(S[:, 0:256], q, kn[rows, c % 2, k0:k0 + 256], start=True, stop=True)
                        mm = pe.matmul(S[:, 256:384], q, ctx_k[rows, c, :], start=True, stop=True)
                    else:
                        mm = pe.matmul(S[:, 0:P], qn[rows, c % 2, LAT:T], kn[rows, c % 2, LAT:T], start=True, stop=True)
                    mm.then_inc(scores_made, 1)

                def turn_probs(c, u):
                    n = l * NU + c * UNITS + u
                    pe.wait_ge(prob_made, n + 1)
                    pe.wait_ge(pt_free, n)
                    if c == u == 0:
                        claim("P", "n2")
                    pr = prob[:, u % 2, :]
                    for i in range(3 if u % 5 < CTX_UNIT else 1):
                        mm = pe.transpose(PT[:, i * P:(i + 1) * P], pr[:, i * P:(i + 1) * P], ident)
                    mm.then_inc(pt_full, 1)

                def values(c, u):
                    e, b = u // 5, u % 5
                    pe.wait_ge(pt_free, l * NU + c * UNITS + u + 1)
                    if u == 0:
                        pe.wait_ge(free["X"], after("X", ("vtr", c, 1), l))
                    claim("O", ("pv", c, u))
                    vt = v_tok[c % 2]
                    if b < CTX_UNIT:
                        for i, grp in enumerate(BLOCK_GROUPS[b]):
                            pe.matmul(O[:, 0:64], probT[:, u % 2, i * P:(i + 1) * P], vt[:, grp, 64 * e:64 * e + 64],
                                      start=i == 0, stop=False)
                        mm = pe.matmul(O[:, 0:64], probT[:, u % 2, 256:384], ctx_v[:, (2 * c + e) * 64:(2 * c + e + 1) * 64],
                                       start=False, stop=True)
                    else:
                        mm = pe.matmul(O[:, 0:64], probT[:, u % 2, 0:P], vt[:, 7, 64 * e:64 * e + 64], start=True, stop=True)
                    mm.then_inc(full["O"], 1)

                def gla_scores(j):
                    pe.wait_ge(kk_made, l * NP + j + 1)
                    pe.wait_ge(qh_made, (l * NP + j + 1) * 2)
                    claim("S", ("sc", j))
                    for d in range(2):
                        for ch in range(2):
                            for i in range(4):
                                t0 = ch * CHUNK + i * SUB
                                mm = pe.matmul(S[ch * CHUNK:(ch + 1) * CHUNK, d * 256 + i * 64:d * 256 + i * 64 + 64],
                                               kk[:, j % 2, d, ch, i, :], q_heads[:, d, :, t0:t0 + SUB],
                                               start=True, stop=True)
                    mm.then_inc(full["S"], 1)

                def gla_outs(j):
                    pe.wait_ge(qi_made, l * 2 + 2)
                    pe.wait_ge(sh_made, (l * NP + j + 1) * 4)
                    pe.wait_ge(att_made, l * NP + j + 1)
                    for ch, b in enumerate("OX"):
                        claim(b, ("go", j))
                        rows = slice(ch * CHUNK, (ch + 1) * CHUNK)
                        toks = slice(j * P + ch * CHUNK, j * P + (ch + 1) * CHUNK)
                        for hp in range(2):
                            region = bank[b][:, hp * CHUNK:(hp + 1) * CHUNK]
                            for d in range(2):
                                pe.matmul(region, s_heads[:, d, ch, hp * P:(hp + 1) * P], kq[:, d, toks],
                                          start=d == 0, stop=False)
                            for e in range(2):
                                hh = 2 * hp + e
                                mm = pe.matmul(
                                    bank[b][64 * e:64 * e + 64, hp * CHUNK:(hp + 1) * CHUNK],
                                    v_la[rows, j, hh * 64:hh * 64 + 64],
                                    att[rows, j % 2, :].rearrange("p (i h t) -> p i h t", i=4, h=4)[:, :, hh, :],
                                    start=False, stop=True)
                        mm.then_inc(full[b], 1)

                for g in range(STEPS):
                    at, end = product_at(g), product_at(g + 1)
                    while at < end:
                        n = at // MMS
                        stop_at = min(end, (n + 1) * MMS)
                        t = T_PAIR + n
                        if at % MMS == 0:
                            ready(t)
                        if g == 3 and stop_at == end:
                            gemm(t % 2, h(h_hi), h(h_lo), at - n * MMS, stop_at - n * MMS - 2)
                            at = stop_at - 2
                            for b, name in (("S", "ufa"), ("P", "ufb"), ("O", "uba"), ("X", "ubb")):
                                claim(b, name)
                        gemm(t % 2, h(h_hi), h(h_lo), at - n * MMS, stop_at - n * MMS)
                        at = stop_at
                    if g == 0:
                        pe.wait_ge(acc_free[(T_V + 1) % 2], acc_uses(l, T_V + 1) + 1)
                        transposes("O", "va1", [vT[:, n * P:(n + 1) * P] for n in range(4)])
                        transposes("X", "va1", [vT[:, 4 * P:5 * P]])
                    if g == 2:
                        pe.wait_ge(kd_made, l * 2 + 2)
                        transposes("S", "kdf", [zl[:, 0, n * P:(n + 1) * P] for n in range(4)])
                        transposes("P", "kdp", [zl[:, d, 4 * P:5 * P] for d in range(2)])
                        transposes("O", "kdb", [zl[:, 1, n * P:(n + 1) * P] for n in range(4)])
                    if g == 3:
                        for d, ch, b in ((0, 0, "S"), (0, 1, "P"), (1, 0, "O"), (1, 1, "X")):
                            rows = slice(ch * CHUNK, (ch + 1) * CHUNK)
                            for j in range(NP):
                                for hh in range(4):
                                    mm = pe.matmul(bank[b][32 * hh:32 * hh + 32, j * CHUNK:(j + 1) * CHUNK],
                                                   kdT[rows, d, j, 32 * hh:32 * hh + 32],
                                                   v_la[rows, j, hh * 64:hh * 64 + 64], start=True, stop=True,
                                                   tile_position=(ch * CHUNK, 32 * hh))
                            mm.then_inc(full[b], 1)
                    for j in gla_scores_at(g):
                        gla_scores(j)
                    for j in gla_outs_at(g):
                        gla_outs(j)
                    for c, u in units_at(g, 0):
                        scores(c, u)
                    for c, u in units_at(g, 1):
                        turn_probs(c, u)
                    for c, u in units_at(g, 2):
                        values(c, u)
                    for name in x_fills_at(g):
                        kind, i, n = name if len(name) == 3 else (name[0], name[1], 0)
                        if kind == "oT":
                            pe.wait_ge(free["O"], after("O", ("pv", i, 5 + n), l))
                            transposes("X", name, [o_tok[:, n, :]])
                        if kind == "vtr":
                            tv = T_PAIR + 3 * i + 2
                            pe.wait_ge(acc_free[tv % 2], acc_uses(l, tv) + 1)
                            src = [vT[:, col * GR:col * GR + P] for col in V_GROUPS] + [vT[:, LAT:T]]
                            transposes("X", name, src[4 * n:4 * n + 4])
                        if kind in ("qsum", "ksum", "gsum"):
                            if kind == "gsum":
                                pe.wait_ge(gla_sq, l * 2 + i + 1)
                            else:
                                t = T_PAIR + 3 * i + (kind == "ksum")
                                pe.wait_ge(acc_free[t % 2], acc_uses(l, t) + 1)
                            claim("X", name)
                            pe.matmul(X[:, 0:HALF], blocks, root[:, halves[n]], start=True, stop=True).then_inc(full["X"], 1)
                        if kind == "pool":
                            pe.wait_ge(pool_d, l * 2 + i + 1)
                            claim("X", name)
                            pe.matmul(X[:, 0:HALF], wpool[:, i, :], root[:, halves[n]], start=True, stop=True
                                      ).then_inc(full["X"], 1)

                def stage(start, tiles, hi, lo, kts=KT, wait_h=None, inputs=None):
                    with pe.Fori(0, tiles // 2) as i:
                        if inputs:
                            pe.wait_ge(*inputs)
                        for p in range(2):
                            pe.wait_ge(lo_made[p], slot_uses(l, start) + i + 1)
                            pe.wait_ge(acc_free[p], acc_uses(l, start + p) + i)
                            gemm(p, h(hi), h(lo), kts=kts, wait_h=wait_h)

                stage(T_OUT, KT, y_hi, y_lo, inputs=(free["X"], (l + 1) * len(FILLS["X"])))
                norm(1)
                made = 0
                for chunk, (n, start) in enumerate(zip(FF_CHUNKS, FF_START)):
                    stage(start, 2 * n, h_hi, h_lo, wait_h=None if chunk else lambda k: l * 16 + 8 + k + 1)
                    made += n
                    stage(start + 2 * n, KT, y_hi, y_lo, kts=n, inputs=(hid_lo, l * NHID + made))


def layout(i):
    import numpy as np

    f = np.float32
    a = {}

    def tiles(w):
        k, m = w.shape
        return w.reshape(k // P, P, m // P, P).transpose(2, 1, 0, 3).reshape(m // P, P, k)

    xs = np.concatenate([i["x_sample"][0], i["x_prompt"][0]], 0)
    a["x"] = xs.T.reshape(KT, P, T).transpose(1, 0, 2)
    a["cond"] = np.stack([i["c"][0], i["c_ctx"]], 1).reshape(KT, P, 2).transpose(1, 0, 2)
    a["w_ada"] = np.concatenate([tiles(i["w_ada"][l]) for l in range(DEPTH)], 0)
    a["b_ada"] = i["b_ada"].reshape(DEPTH * NMOD, P).T
    w = np.zeros((DEPTH * NT, P, KT * P), f)
    cuts = np.cumsum([256, 512, 512, 512, 128, 128, 256, 256, 16])
    for l in range(DEPTH):
        pool, q, k, v, ql, kl, vl, g, lf, lb = np.split(i["w_in"][l], cuts, 1)
        lr = np.concatenate([lf, lb, np.zeros((D, P - LRW), f)], 1)
        t = w[l * NT:(l + 1) * NT]
        t[0, :, :KT // 2 * P] = tiles(lr[:D // 2])[0]
        t[1, :, :KT // 2 * P] = tiles(lr[D // 2:])[0]
        t[T_K], t[T_Q] = tiles(kl)[0], tiles(ql)[0]
        t[T_V:T_V + 2] = tiles(vl)
        for s, m in enumerate((q, k, v)):
            t[T_PAIR + s:T_G:3] = tiles(m)
        t[T_G:T_POOL] = tiles(g)
        t[T_POOL:T_OUT] = tiles(pool)
        t[T_OUT:T_FF] = tiles(i["w_out"][l])
        win, wout = tiles(i["w_ffn_in"][l]), i["w_ffn_out"][l]
        at, done = T_FF, 0
        for n in FF_CHUNKS:
            t[at:at + 2 * n:2] = win[done:done + n]
            t[at + 1:at + 2 * n:2] = win[NHID + done:NHID + done + n]
            t[at + 2 * n:at + 2 * n + KT, :, :n * P] = tiles(wout[done * P:(done + n) * P])
            at, done = at + 2 * n + KT, done + n
    a["w"] = w
    twice = lambda v: np.concatenate([v, v])
    cols = np.zeros((DEPTH, NSMALL, P), f)
    for l in range(DEPTH):
        cols[l, C_G1:C_G1 + KT] = i["norm1_gain"][l].reshape(KT, P)
        cols[l, C_G2:C_G2 + KT] = i["norm2_gain"][l].reshape(KT, P)
        cols[l, C_PS:C_PS + 2] = i["pool_scale"][l].reshape(2, P)
        cols[l, C_QG], cols[l, C_KG] = twice(i["q_norm_gain"][l]), twice(i["k_norm_gain"][l])
        cols[l, C_BF], cols[l, C_BB] = i["b_gate_f"][l], i["b_gate_b"][l]
        cols[l, C_LG] = twice(i["gla_norm_gain"][l])
    a["small"] = cols.transpose(2, 0, 1)
    wg = np.zeros((DEPTH, LRW, 2 * P), f)
    wg[:, :16, :P], wg[:, 16:, P:] = i["w_gate_f"], i["w_gate_b"]
    a["wgate"] = wg
    wp = np.zeros((DEPTH, P, 2, P), f)
    for g in range(4):
        r = slice(g % 2 * 64, g % 2 * 64 + 64)
        wp[:, r, g // 2, r] = i["w_pool"][:, g]
    a["wpool"] = wp
    a["state"] = np.stack([i["state_gla_fwd"][0], i["state_gla_bwd"][0]], 1).reshape(DEPTH, 2, P, CHUNK).transpose(2, 0, 1, 3)
    a["ctx_k"] = i["cache_na_k"][0].reshape(DEPTH, PAIRS, 2, P, 64).transpose(0, 2, 4, 1, 3).reshape(DEPTH, P, PAIRS, P)
    a["ctx_v"] = i["cache_na_v"][0].transpose(0, 2, 1, 3).reshape(DEPTH, P, 512)
    rb = i["rel_bias"].reshape(DEPTH * 8, 15 * 31)
    rb = np.concatenate([rb, np.full((DEPTH * 8, 1), -1e30, f), np.zeros((DEPTH * 8, 1), f)], 1)
    where = np.full((P, 3, 384), 15 * 31 + 1)
    for kind, blk in ((0, 0), (1, 1), (2, 3)):
        c, r = np.divmod(np.arange(P), GR)
        c2, r2 = np.divmod(np.arange(256), GR)
        c, c2 = c + 16 * blk, c2 + KEY_START[blk]
        lo = np.clip(c - 8, 0, GW - 16)[:, None]
        inside = (c2[None] >= lo) & (c2[None] < lo + 16)
        at = (r2[None] - r[:, None] + 7) * 31 + c2[None] - c[:, None] + 15
        where[:, kind, :256] = np.where(inside, at, 15 * 31)
    a["bias"] = rb[:, where].reshape(DEPTH, PAIRS, 2, P, 3, 384)
    eye, p = np.eye(P, dtype=f), np.arange(P)
    swap = np.zeros((P, P), f)
    low = p % 16 < 8
    swap[np.where(low, p + 8, p - 8), p] = np.where(low, -1, 1)
    a["mats"] = np.stack([eye, (p[:, None] // 64 == p // 64).astype(f), np.ones((P, P), f), swap], 1)
    tok = np.arange(LAT)
    inv = (f(10000.0) ** (-np.arange(0, 16, 2, dtype=f) / f(16))).astype(f)
    pos = np.where((p % 32 < 16)[:, None], (tok // GW)[None], (tok % GW)[None]).astype(f)
    ang = pos * inv[p % 8][:, None]
    rope = np.zeros((P, 2, T), f)
    rope[:, 0, LAT:] = 1
    rope[:, 0, :LAT], rope[:, 1, :LAT] = np.cos(ang), np.sin(ang)
    a["rope"] = rope
    s = (p % CHUNK)[:, None]
    tt = np.arange(4)[:, None, None] * SUB + np.zeros((1, 4, 1), int) + np.arange(SUB)
    tt = tt.reshape(1, 256)
    a["causal"] = np.concatenate([s <= tt, s >= tt], 1).astype(f)
    a["heads4"] = (p[:, None] // 32 == np.arange(4)).astype(f)
    win = np.array([[2, 4], [8, 16]])[:, p // 64].T
    a["inv_w"] = (1.0 / win).astype(f)
    edges = np.ones((P, 2, 2, 2, 8), f)
    for st, n in enumerate((LAT, CTX)):
        for e, ts in enumerate((np.arange(8), np.arange(n - 8, n))):
            half = win[:, :, None] // 2
            count = np.minimum(ts + half, n) - np.maximum(ts - half, 0)
            edges[:, :, st, e, :] = win[:, :, None] / count
    a["edges"] = edges
    return {n: np.ascontiguousarray(v) for n, v in a.items()}


_OUTS = {"x": (P, KT, T), "k": (DEPTH, PAIRS, P, CTX), "v": (DEPTH, PAIRS, P, CTX), "s": (DEPTH, P, 2, CHUNK)}


def kernel(**inputs):
    import numpy as np
    import concourse.bacc as bacc
    from concourse.bass_utils import run_bass_kernel_spmd

    arrays = layout({n: np.asarray(v) for n, v in inputs.items()})
    nc = bacc.Bacc("TRN2", target_bir_lowering=False, num_devices=1)
    a = {n: nc.dram_tensor(f"in_{n}", v.shape, mybir.dt.from_np(v.dtype), kind="ExternalInput").ap() for n, v in arrays.items()}
    out = {n: nc.dram_tensor(f"out_{n}", s, F32, kind="ExternalOutput").ap() for n, s in _OUTS.items()}
    build(nc, a, out)
    r = run_bass_kernel_spmd(nc, [{f"in_{n}": v for n, v in arrays.items()}], core_ids=[0]).results[0]
    y = r["out_x"].transpose(1, 0, 2).reshape(D, T).T
    k, v = (r[f"out_{n}"].reshape(1, DEPTH, 8, 64, CTX).transpose(0, 1, 2, 4, 3) for n in "kv")
    s = r["out_s"].reshape(1, DEPTH, 4, 32, 2, CHUNK)
    return y[LAT:][None], y[:LAT][None], k, v, s[:, :, :, :, 0], s[:, :, :, :, 1]
```

```python
from contextlib import ExitStack

import concourse.bass as bass
from concourse import mybir

F32 = mybir.dt.float32
F32R = mybir.dt.float32r
ALU = mybir.AluOpType
ACT = mybir.ActivationFunctionType

P = 128
DEPTH = 2
D = 1024
KT = D // P
LAT, CTX = 512, 128
T = LAT + CTX
HALF = T // 2
GW, GR = 64, 8
EPS = 1e-6
PAIRS = 4
FF_CHUNKS = (8, 8, 6)
SUB = 16
CHUNK = 64
NCH = T // CHUNK
NP = T // P
LIMIT = 40.0
TAU = 16.0

T_LR, T_K, T_Q, T_V, T_PAIR = 0, 2, 3, 4, 6
T_G = T_PAIR + 3 * PAIRS
T_POOL = T_G + 2
T_OUT = T_POOL + 2
T_FF = T_OUT + KT
NT = T_FF + sum(2 * n + KT for n in FF_CHUNKS)
WN = NT // 2
NPAR = 9
LRW = 32
NHID = sum(FF_CHUNKS)
NMOD = 48
SHIFT1, SCALE1, GATE1, SHIFT2, SCALE2, GATE2 = range(0, NMOD, KT)
NMID = GATE1 + KT
NROWS = 16
ROW_SLOTS, COL_SLOTS = 8, 2

C_G1, C_G2, C_PS, C_QG, C_KG, C_BF, C_BB, C_LG = 0, 8, 16, 18, 19, 20, 21, 22
NSMALL = 23

V_GROUPS = (0, 16, 8, 24, 40, 32, 48)
BLOCK_GROUPS = ((0, 1), (2, 3), (3, 4), (5, 6))
KEY_START = (0, 8, 24, 32)
BIAS_KIND = (0, 1, 1, 2)

HEAD_STEPS, TAIL_STEPS = 10, 14
GEMM_STEPS = HEAD_STEPS * PAIRS + TAIL_STEPS
STEPS = GEMM_STEPS + 3
MMS = 6 * KT
UNITS = 10
NU = PAIRS * UNITS
CTX_UNIT = 4


def product_at(step):
    if step <= HEAD_STEPS * PAIRS:
        return step * 3 * MMS // HEAD_STEPS
    return min(3 * PAIRS * MMS + (step - HEAD_STEPS * PAIRS) * 4 * MMS // TAIL_STEPS, (3 * PAIRS + 4) * MMS)


def tiles_done(step):
    return [n for n in range(3 * PAIRS + 4) if product_at(step - 1) < (n + 1) * MMS <= product_at(step)] if step else []


def units_at(step, lag):
    n = step - HEAD_STEPS - 1 - lag
    return [(n // UNITS, n % UNITS)] if 0 <= n < NU else []


def gla_scores_at(step):
    return [j for j in range(NP) if step == 4 + j]


def gla_outs_at(step):
    return [j for j in range(NP) if step == 5 + j]


def x_fills_at(step):
    out = [("go", j) for j in gla_outs_at(step)]
    out += [("oT", c, b) for c in range(PAIRS) for b in range(5) if step == 10 * c + 19 + b]
    out += [("vtr", c, i) for c in range(PAIRS) for i in range(2) if step == 10 * c + 10 + i]
    out += [("gsum", i, h) for i in range(2) for h in range(2) if step == 10 * i + 11 + h]
    out += [("qsum", c, h) for c in range(PAIRS) for h in range(2) if step == 10 * c + 4 + h]
    out += [("ksum", c, h) for c in range(PAIRS) for h in range(2) if step == 10 * c + 7 + h]
    out += [("pool", i, h) for i in range(2) for h in range(2) if step == 51 + 3 * i + h]
    return out


FILLS = {
    "S": ["n1", "zf", "rk", "va0", "kdf", "ufa"] + [("sc", j) for j in range(NP)]
    + ["n2"],
    "P": ["n1", "zf", "rk", "va0", "kdp", "ufb", "n2"],
    "O": ["zb", "rq", "va1", "kdb", "uba"] + [("go", j) for j in range(NP)]
    + [("pv", c, u) for c in range(PAIRS) for u in range(UNITS)],
    "X": ["zb", "rq", "va1", "ubb"] + [f for g in range(STEPS) for f in x_fills_at(g)],
}
ROOTS = ["n1", ("q", 0), ("k", 0), ("g", 0), ("q", 1), ("k", 1), ("g", 1), ("q", 2), ("k", 2), ("q", 3), ("k", 3), "n2"]
NR = len(ROOTS)


def before(bank, name, l):
    return l * len(FILLS[bank]) + FILLS[bank].index(name)


def after(bank, name, l):
    return before(bank, name, l) + 1


def norms(l, name):
    return l * (NR - 2) + ROOTS.index(name) - 1


def slot_uses(l, t):
    return l * WN + t // 2


def acc_uses(l, t):
    return l * WN + t // 2 if t % 2 else l * (WN - 1) + (t - 2) // 2


class Count:

    def __init__(self, per_layer):
        self.per_layer, self.n = per_layer, 0

    def up(self, l):
        self.n += 1
        return l * self.per_layer + self.n


DVE_STEPS, ACT_STEPS = 148, 24


def build(nc, a, out):
    ctx = ExitStack()
    with ctx:
        def sb(name, shape, dt=F32, stack=ctx):
            return stack.enter_context(nc.sbuf_tensor(name, shape, dt))

        def sem(name):
            return ctx.enter_context(nc.semaphore(name))

        x = sb("x", [P, KT, T])
        h_hi, h_lo = sb("h_hi", [P, KT, T], F32R), sb("h_lo", [P, KT, T], F32R)
        raw = [sb(f"w_raw{p}", [P, KT * P]) for p in range(2)]
        w_hi = [sb(f"w_hi{p}", [P, KT * P], F32R) for p in range(2)]
        w_lo = [sb(f"w_lo{p}", [P, KT * P], F32R) for p in range(2)]
        mats = sb("mats", [P, 4, P])
        ident, blocks, ones, swap = (mats[:, i, :] for i in range(4))
        rope = sb("rope", [P, 2, T])
        causal = sb("causal", [P, 512])
        heads4 = sb("heads4", [P, 4])
        edges = sb("edges", [P, 2, 2, 2, 8])
        inv_w = sb("inv_w", [P, 2])
        small_all = sb("small_all", [P, DEPTH, NSMALL])
        b_ada = sb("b_ada", [P, NMID + DEPTH * NMOD])
        b_turn = sb("b_turn", [P, NMOD])
        mods_next = sb("mods_next", [P, NMID, 2])
        small = sb("small", [P, NSMALL])
        mods = sb("mods", [P, NMOD, 2])
        gain = sb("gain", [P, 2, KT, 2])
        state_in = sb("state_in", [P, DEPTH, 2, CHUNK])
        cond = sb("cond", [P, KT, 2])
        wgate = sb("wgate", [LRW, 2 * P])
        wpool = sb("wpool", [P, 2, P])
        PADT = T + 32
        LAT0, CTX0 = 8, LAT + 24
        tmp = sb("tmp", [P, 2, PADT])
        mean = sb("mean", [P, PADT])
        root = sb("root", [P, T])
        with ExitStack() as first:
            lrT = sb("lrT", [LRW, T], F32, first)
        rstd = sb("rstd", [P, T])
        vT = sb("vT", [P, T])
        with ExitStack() as first:
            cond_rows = sb("cond_rows", [P, 2, D], F32, first)
            mod_w = [sb(f"mod_w{p}", [P, D], F32, first) for p in range(2)]
        qn, kn = sb("qn", [P, 2, T]), sb("kn", [P, 2, T])
        bias = [sb(f"bias{e}", [P, 3, 384]) for e in range(2)]
        ctx_k, ctx_v = sb("ctx_k", [P, PAIRS, P]), sb("ctx_v", [P, 512])
        gla_o = sb("gla_o", [P, 2, T])
        row_stat = sb("row_stat", [P, 3, 4])
        decay = sb("decay", [P, 2, NCH])
        final = sb("final", [P, 2, CHUNK])

        with ExitStack() as first:
            ada = [sb(f"w_ada{s}", [P, KT * P], F32, first) for s in range(ROW_SLOTS + COL_SLOTS)]
        with ExitStack() as first:
            kq = sb("kq", [P, 2, T], F32, first)
            kr = sb("kr", [P, T], F32, first)
            qr = sb("qr", [P, T], F32, first)
            z = sb("z", [P, 2, T], F32, first)
            zl = sb("zl", [P, 2, T], F32, first)
            bcum = sb("bcum", [P, 2, T], F32, first)
            kdT = sb("kdT", [P, 2, NP, P], F32, first)
            kk = sb("kk", [P, 2, 2, 2, 4, CHUNK], F32, first)
        y_hi, y_lo = sb("y_hi", [P, KT, T], F32R), sb("y_lo", [P, KT, T], F32R)
        with ExitStack() as first:
            q_heads = sb("q_heads", [P, 2, 4, P], F32, first)
        gate = sb("gate", [P, 2, T])
        with ExitStack() as first:
            s_heads = sb("s_heads", [P, 2, 2, 4 * CHUNK], F32, first)
        v_tok1 = sb("v_tok1", [P, 8, P])
        v_tok = [sb("v_tok0", [P, 8, P]), v_tok1]
        with ExitStack() as first:
            neg_s = sb("neg_s", [P, 384], F32, first)
            prob = sb("prob", [P, 2, 384], F32, first)
            probT = sb("probT", [P, 2, 384], F32, first)
            o_tok = sb("o_tok", [P, NP, P], F32, first)
        v_la = sb("v_la", [P, NP, 256])
        states = sb("states", [P, 2, NCH, CHUNK])
        att = sb("att", [P, 2, 256])

        acc = [ctx.enter_context(nc.psum_tensor(f"acc{p}", [P, 2, 512], F32)) for p in range(2)]
        bank = {n: ctx.enter_context(nc.psum_tensor(f"bank_{n}", [P, 512], F32)) for n in "SP"}
        pair = ctx.enter_context(nc.psum_tensor("banks_OX", [P, 2, 512], F32))
        bank |= {n: pair[:, i, :] for i, n in enumerate("OX")}
        products = pair[:].rearrange("p b n -> p (b n)")
        S, PT, O, X = (bank[n] for n in "SPOX")

        x_in, par_in, cond_in, cond_made, layer_in = (sem(n) for n in ("x_in", "par_in", "cond_in", "cond_made", "layer_in"))
        ada_in = [sem(f"ada_in{s}") for s in range(ROW_SLOTS + COL_SLOTS)]
        ada_cols_used = sem("ada_cols_used")
        rows_in, rows_made, mod_used, mod_in = sem("rows_in"), sem("rows_made"), sem("mod_used"), [sem(f"mod_in{p}") for p in range(2)]
        raw_in, hi_made, lo_made, tile_done, acc_free, bias_in, k_out = (
            [sem(f"{n}{p}") for p in range(2)]
            for n in ("raw_in", "hi_made", "lo_made", "tile_done", "acc_free", "bias_in", "k_out"))
        full = {n: sem(f"full_{n}") for n in "SPOX"}
        free = {n: sem(f"free_{n}") for n in "SPOX"}
        pt_full, pt_free = sem("pt_full"), sem("pt_free")
        norm_sq, sq_used = sem("norm_sq"), sem("sq_used")
        gla_sq, root_made, norm_done = sem("gla_sq"), sem("root_made"), sem("norm_done")
        scaled, h_hi_made, h_made = sem("scaled"), sem("h_hi_made"), sem("h_made")
        log_made, args_made, rope_made, exps_made = (sem(n) for n in ("log_made", "args_made", "rope_made", "exps_made"))
        kd_made, qi_made, qe_made = sem("kd_made"), sem("qi_made"), sem("qe_made")
        kk_arg, kk_exp, kk_made = sem("kk_arg"), sem("kk_exp"), sem("kk_made")
        qh_made, sh_made, att_made = sem("qh_made"), sem("sh_made"), sem("att_made")
        scores_made, biased, prob_made = sem("scores_made"), sem("biased"), sem("prob_made")
        pool_d, gate_exp, gated, gated_hi = (sem(n) for n in ("pool_d", "gate_exp", "gated", "gated_hi"))
        hid_hi, hid_lo = sem("hid_hi"), sem("hid_lo")
        dve_step, act_step = sem("dve_step"), sem("act_step")
        ctx_in, v_out, s_out, y_out = sem("ctx_in"), sem("v_out"), sem("s_out"), sem("y_out")
        from_one = [*acc_free, *tile_done, *lo_made, *k_out, *free.values(), pt_free, norm_done, hid_lo, prob_made,
                    biased, v_out, s_out]

        halves = (slice(0, HALF), slice(HALF, T))

        def two(ap):
            return ap.rearrange("p (h n) -> p h n", h=2)

        def acc_all(p):
            return acc[p][:, :, 0:HALF]

        def grid(ap, col, width):
            return ap[:, 0:LAT].rearrange("p (r w) -> p r w", r=GR)[:, :, col:col + width]

        def by_column(ap):
            lat = ap[:, 0:LAT].rearrange("p (w r) -> p w r", r=GR)
            return lat[:, :, 0:HALF // GW], lat[:, :, HALF // GW:GR], ap[:, LAT:T]

        def acc_parts(p):
            return (acc[p][:, 0, 0:HALF].rearrange("p (r w) -> p w r", w=GW),
                    acc[p][:, 1, 0:LAT - HALF].rearrange("p (r w) -> p w r", w=GW), acc[p][:, 1, LAT - HALF:HALF])

        def wide(ap, n):
            return ap.unsqueeze(2).broadcast_to([P, ap.shape[1], n])

        STREAMS = ((0, slice(0, LAT)), (1, slice(LAT, T)))
        PIECES = ((0, 0, 0, HALF), (0, 1, 0, LAT - HALF), (1, 1, LAT - HALF, HALF))

        def kts_of(t):
            return KT // 2 if t < T_K else KT

        FF_START, t0 = [], T_FF
        for n in FF_CHUNKS:
            FF_START.append(t0)
            t0 += 2 * n + KT

        block = ctx.enter_context(nc.Block())

        @block.sync
        def _(sp):
            for s in from_one:
                sp.sem_inc(s, 1)
            sp.dma_start(cond[:], a["cond"]).then_inc(cond_in, 16)
            sp.dma_start(cond_rows[:], a["cond_rows"]).then_inc(rows_in, 16)

            def load_row(n):
                if n >= ROW_SLOTS:
                    sp.wait_ge(mod_used, 2 * (n - ROW_SLOTS + 1))
                sp.dma_start(ada[n % ROW_SLOTS][:], a["w_ada"][n]).then_inc(ada_in[n % ROW_SLOTS], 16)

            for n in range(NMID - NROWS):
                load_row(2 * n)
                load_row(2 * n + 1)
                if n >= COL_SLOTS:
                    sp.wait_ge(ada_cols_used, n - COL_SLOTS + 1)
                slot = ROW_SLOTS + n % COL_SLOTS
                sp.dma_start(ada[slot][:], a["w_ada"][NROWS + n]).then_inc(ada_in[slot], 16)
                if n == 2:
                    sp.dma_start(x[:], a["x"]).then_inc(x_in, 16)
                    for m, t in (("mats", mats), ("b_ada", b_ada), ("small", small_all), ("rope", rope),
                                 ("causal", causal), ("heads4", heads4), ("edges", edges), ("inv_w", inv_w),
                                 ("state", state_in)):
                        sp.dma_start(t[:], a[m]).then_inc(par_in, 16)

            with sp.Fori(0, DEPTH) as l:
                def load(t):
                    sp.wait_ge(lo_made[t % 2], 1 + slot_uses(l, t))
                    n = kts_of(t) * P
                    sp.dma_start(raw[t % 2][:, 0:n], a["w"][l * NT + t, :, 0:n]).then_inc(raw_in[t % 2], 16)

                def load_bias(c, e):
                    sp.wait_ge(biased, 1 + l * NU + (UNITS * (c - 1) + 5 * (e + 1) if c else 0))
                    sp.dma_start(bias[e][:], a["bias"][l, c, e]).then_inc(bias_in[e], 16)

                sp.wait_ge(free["X"], 1 + l * len(FILLS["X"]))
                sp.dma_start(wgate[:], a["wgate"][l]).then_inc(layer_in, 16)
                sp.dma_start(wpool[:], a["wpool"][l]).then_inc(layer_in, 16)
                for t in range(T_OUT):
                    load(t)
                    if t == T_K:
                        sp.wait_ge(free["O"], 1 + l * len(FILLS["O"]))
                        sp.dma_start(ctx_k[:], a["ctx_k"][l]).then_inc(ctx_in, 16)
                        sp.dma_start(ctx_v[:], a["ctx_v"][l]).then_inc(ctx_in, 16)
                        load_bias(0, 0)
                        load_bias(0, 1)
                    if t >= T_PAIR + 6 and t % 3 == 2:
                        c = (t - T_PAIR) // 3 - 1
                        if c < PAIRS:
                            load_bias(c, 0)
                            load_bias(c, 1)
                    for c in range(PAIRS):
                        if t == min(T_PAIR + 3 * c + 5, T_OUT - 1):
                            sp.wait_ge(norm_done, 1 + norms(l, ("k", c)) + 1)
                            sp.dma_start(out["k"][l, c], kn[:, c % 2, LAT:T]).then_inc(k_out[c % 2], 16)
                            tv = T_PAIR + 3 * c + 2
                            sp.wait_ge(acc_free[tv % 2], 1 + acc_uses(l, tv) + 1)
                            sp.dma_start(out["v"][l, c], vT[:, LAT:T]).then_inc(v_out, 16)
                    if t == T_PAIR + 4:
                        sp.wait_ge(free["X"], 1 + after("X", "ubb", l))
                        sp.dma_start(out["s"][l], final[:]).then_inc(s_out, 16)

                def load_mod(p, k):
                    sp.wait_ge(mod_used, 2 * (l * NMOD + NROWS + k - 1))
                    sp.dma_start(mod_w[p][:], a["w_ada"][l * NMOD + NMID + k]).then_inc(mod_in[p], 16)

                def load_next(p, start, i, kts):
                    sp.wait_ge(lo_made[p], 1 + slot_uses(l, start) + i)
                    sp.dma_start(raw[p][:, 0:kts * P], a["w"][l * NT + start + 2 * i + p, :, 0:kts * P]
                                 ).then_inc(raw_in[p], 16)

                for t in range(T_OUT, T_FF):
                    load(t)
                    if t == T_OUT + 1:
                        fills, stores = (l + 1) * len(FILLS["X"]), (l + 1) * 16 * PAIRS // 2
                        sp.wait_ge(free["X"], 1 + fills)
                        sp.wait_ge(k_out[0], 1 + stores)
                        sp.wait_ge(k_out[1], 1 + stores)
                        sp.dma_start(cond_rows[:], a["cond_rows"]).then_inc(rows_in, 16)
                        for k in range(2):
                            load_mod(k, k)
                    if t > T_OUT + 1:
                        for k in range(2):
                            load_mod(k, 2 * (t - T_OUT - 1) + k)
                for k in range(2):
                    load_mod(k, 2 * KT - 2 + k)
                k = 2 * KT
                for chunk, (n, start) in enumerate(zip(FF_CHUNKS, FF_START)):
                    with sp.Fori(0, n // 2) as i:
                        for p in range(2):
                            load_next(0, start, 2 * i + p, KT)
                            load_next(1, start, 2 * i + p, KT)
                            if chunk < 2:
                                load_mod(p, k + 2 * i + p)
                    k += n
                    with sp.Fori(0, KT // 2) as i:
                        for p in range(2):
                            load_next(p, start + 2 * n, i, n)
                            if chunk < 2:
                                load_mod(p, k + 2 * i + p)
                    k += KT

            sp.wait_ge(acc_free[0], 1 + DEPTH * (WN - 1))
            sp.wait_ge(acc_free[1], 1 + DEPTH * WN)
            sp.dma_start(out["x"], x[:]).then_inc(y_out, 16)
            for s, n in ((k_out[0], 2), (k_out[1], 2), (v_out, 4), (s_out, 1)):
                sp.wait_ge(s, 1 + 16 * DEPTH * n)
            sp.wait_ge(y_out, 16)

        @block.gpsimd
        def _(pool):
            pool.wait_ge(par_in, 16 * NPAR)
            with pool.Fori(0, DEPTH) as l:
                def low(p, uses, n):
                    pool.wait_ge(hi_made[p], uses + 1)
                    pool.tensor_tensor(w_lo[p][:, 0:n], raw[p][:, 0:n], w_hi[p][:, 0:n].bitcast(F32),
                                       ALU.subtract).then_inc(lo_made[p], 1)

                def by_head(j):
                    if j == 0:
                        pool.wait_ge(qe_made, l * 2 + 2)
                    else:
                        pool.wait_ge(full["S"], after("S", ("sc", j - 1), l))
                    for d in range(2):
                        pool.tensor_tensor(
                            q_heads[:, d], z[:, d, j * P:(j + 1) * P].unsqueeze(1).broadcast_to([P, 4, P]),
                            wide(heads4[:], P), ALU.mult).then_inc(qh_made, 1)
                    if j == 0:
                        pool.wait_ge(free["S"], 1 + after("S", "ufa", l))
                        pool.wait_ge(free["X"], 1 + after("X", "ubb", l))
                    else:
                        pool.wait_ge(full["X"], after("X", ("go", j - 1), l))
                    for d in range(2):
                        for ch in range(2):
                            pool.tensor_tensor(
                                s_heads[:, d, ch].rearrange("p (h n) -> p h n", h=4),
                                states[:, d, 2 * j + ch, :].unsqueeze(1).broadcast_to([P, 4, CHUNK]),
                                wide(heads4[:], CHUNK), ALU.mult).then_inc(sh_made, 1)

                for t in range(T_OUT):
                    low(t % 2, slot_uses(l, t), kts_of(t) * P)
                    if t == T_PAIR + 2:
                        for j in range(NP):
                            by_head(j)
                with pool.Fori(0, (NT - T_OUT) // 2) as i:
                    for p in range(2):
                        low(p, slot_uses(l, T_OUT) + i, KT * P)

        @block.scalar
        def _(act):
            act.wait_ge(cond_in, 16)
            act.activation(cond[:], cond[:], ACT.Silu).then_inc(cond_made, 1)
            act.wait_ge(rows_in, 16)
            act.activation(cond_rows[:], cond_rows[:], ACT.Silu).then_inc(rows_made, 1)
            act.wait_ge(x_in, 16)

            with act.Fori(0, DEPTH) as l:
                steps = Count(ACT_STEPS)

                def link(ins):
                    ins.then_inc(act_step, 1)
                    act.wait_ge(act_step, steps.up(l))

                def high(p, uses, n=KT * P):
                    act.wait_ge(raw_in[p], (uses + 1) * 16)
                    act.wait_ge(tile_done[p], 1 + uses)
                    act.activation(w_hi[p][:, 0:n], raw[p][:, 0:n], ACT.Copy).then_inc(hi_made[p], 1)

                def high_tile(t):
                    high(t % 2, slot_uses(l, t), kts_of(t) * P)

                def inverse_root(waits):
                    for s, n in waits:
                        act.wait_ge(s, 1 + n)
                    link(act.activation(root[:], mean[:, 0:T], ACT.Ln))
                    act.activation(root[:], root[:], ACT.Exp, scale=-0.5).then_inc(root_made, 1)

                def norm(w):
                    for k in range(KT):
                        if w:
                            act.wait_ge(acc_free[k % 2], 1 + acc_uses(l, T_OUT + k) + 1)
                        if k >= 2:
                            act.wait_ge(sq_used, l * 14 + w * 7 + k - 1)
                        act.activation(tmp[:, k % 2, 0:T], x[:, k, :], ACT.Square).then_inc(norm_sq, 1)
                    inverse_root(((free["S"], after("S", ("n1", "n2")[w], l)), (free["P"], after("P", ("n1", "n2")[w], l))))
                    for k in range(KT):
                        act.wait_ge(scaled, l * 16 + w * 8 + k + 1)
                        for s, cols in STREAMS:
                            ins = act.activation(h_hi[:, k, cols], tmp[:, k % 2, cols], ACT.Identity,
                                                 bias=mods[:, (SHIFT1, SHIFT2)[w] + k, s:s + 1])
                        ins.then_inc(h_hi_made, 1)

                def evacuate(t, dst, scale=1.0):
                    act.wait_ge(tile_done[t % 2], 1 + slot_uses(l, t) + 1)
                    return act.activation(two(dst), acc_all(t % 2), ACT.Copy, scale=scale)

                def evacuate_by_column(t, dst):
                    act.wait_ge(tile_done[t % 2], 1 + slot_uses(l, t) + 1)
                    for to, part in zip(by_column(dst), acc_parts(t % 2)):
                        ins = act.activation(to, part, ACT.Copy)
                    return ins

                high_tile(0)
                high_tile(1)
                act.wait_ge(acc_free[0], 1 + l * (WN - 1))
                act.wait_ge(acc_free[1], 1 + l * WN)
                norm(0)
                high_tile(T_K)
                high_tile(T_Q)
                evacuate(T_K, kq[:, 0, :]).then_inc(acc_free[T_K % 2], 1)
                high_tile(T_V)
                for d, (b, n) in enumerate((("P", "zf"), ("X", "zb"))):
                    act.wait_ge(free[b], 1 + after(b, n, l))
                    link(act.activation(zl[:, d, :], z[:, d, :], ACT.Abs))
                    link(act.activation(zl[:, d, :], zl[:, d, :], ACT.Exp, scale=-1.0))
                    act.activation(zl[:, d, :], zl[:, d, :], ACT.Ln, bias=1.0).then_inc(log_made, 1)
                evacuate(T_Q, kq[:, 1, :], 32 ** -0.5).then_inc(acc_free[T_Q % 2], 1)
                high_tile(T_V + 1)
                act.wait_ge(v_out, 1 + 16 * 4 * l)
                evacuate(T_V, vT[:]).then_inc(acc_free[T_V % 2], 1)
                high_tile(T_PAIR)
                for i, buf in enumerate((zl, z)):
                    for d in range(2):
                        act.wait_ge(args_made, l * 2 + d + 1)
                        act.activation(buf[:, d, :], buf[:, d, :], ACT.Exp, scale=1.0 / TAU).then_inc(exps_made, 1)
                for d, end in ((0, CHUNK - 1), (1, 0)):
                    act.activation(decay[:, d, :], bcum[:, d, end:T:CHUNK], ACT.Exp, scale=1.0 / TAU).then_inc(exps_made, 1)
                act.wait_ge(full["P"], after("P", "va0", l))
                evacuate(T_V + 1, vT[:]).then_inc(acc_free[(T_V + 1) % 2], 1)
                high_tile(T_PAIR + 1)
                act.wait_ge(rope_made, l + 1)
                for d in range(2):
                    act.activation(kq[:, d, :], bcum[:, d, :], ACT.Exp, scale=1.0 / TAU).then_inc(exps_made, 1)

                for g in range(STEPS):
                    for j in range(NP):
                        if g == 3 + j:
                            act.wait_ge(kk_arg, l * NP + j + 1)
                            act.activation(kk[:, j % 2], kk[:, j % 2], ACT.Exp, scale=1.0 / TAU).then_inc(kk_exp, 1)
                    for name in x_fills_at(g - 1):
                        if name[0] in ("qsum", "ksum", "gsum") and name[2]:
                            inverse_root(((free["X"], after("X", name, l)),))
                    for n in tiles_done(g):
                        t = T_PAIR + n
                        if t + 2 < T_OUT:
                            high_tile(t + 2)
                        else:
                            high(t % 2, slot_uses(l, t + 2))
                        if n < 3 * PAIRS and n % 3 < 2:
                            c = n // 3
                            if n % 3:
                                act.wait_ge(k_out[c % 2], 1 + 16 * (l * 2 + c // 2))
                            row = (qn, kn)[n % 3][:, c % 2, :]
                            link(evacuate_by_column(t, row))
                            act.wait_ge(norm_done, 1 + norms(l, ("qk"[n % 3], c)))
                            act.activation(root[:], row, ACT.Square).then_inc(acc_free[t % 2], 1)
                        elif n < 3 * PAIRS:
                            c = n // 3
                            act.wait_ge(v_out, 1 + 16 * (l * 4 + c))
                            act.wait_ge(full["X"], after("X", ("vtr", c - 1, 1) if c else "va1", l))
                            evacuate_by_column(t, vT[:]).then_inc(acc_free[t % 2], 1)
                        elif t < T_POOL:
                            i = t - T_G
                            evacuate(t, gate[:, i, :]).then_inc(acc_free[t % 2], 1)
                            act.wait_ge(acc_free[t % 2], 1 + acc_uses(l, t) + 1)
                            act.activation(tmp[:, i, 0:T], gate[:, i, :], ACT.Exp, scale=-1.0).then_inc(gate_exp, 1)
                    for i in range(2):
                        if g == 10 * i + 11:
                            act.wait_ge(free["X"], 1 + after("X", ("go", NP - 1), l))
                            act.wait_ge(norm_done, 1 + norms(l, ("g", i)))
                            act.activation(root[:], gla_o[:, i, :], ACT.Square).then_inc(gla_sq, 1)
                    for c, u in units_at(g, 1):
                        n = l * NU + c * UNITS + u
                        w = 384 if u % 5 < CTX_UNIT else P
                        act.wait_ge(biased, 1 + n + 1)
                        act.activation(prob[:, u % 2, 0:w], neg_s[:, 0:w], ACT.Exp, bias=row_stat[:, 0, u % 4:u % 4 + 1],
                                       scale=-1.0, accum_out=row_stat[:, 1, u % 4:u % 4 + 1]).then_inc(prob_made, 1)
                    for c, u in units_at(g, 2):
                        n = l * NU + c * UNITS + u
                        w = 384 if u % 5 < CTX_UNIT else P
                        act.wait_ge(pt_full, n + 1)
                        if c or u >= 2:
                            m = c * UNITS + u - 2
                            act.wait_ge(full["O"], after("O", ("pv", m // UNITS, m % UNITS), l))
                        act.activation(probT[:, u % 2, 0:w], PT[:, 0:w], ACT.Copy).then_inc(pt_free, 1)
                    for i in range(2):
                        if g == 50 + i:
                            act.wait_ge(gated, l * 2 + i + 1)
                            act.activation(y_hi[:, 6 + i, :], gla_o[:, i, :], ACT.Copy).then_inc(gated_hi, 1)

                def high_pairs(start, tiles, last=False):
                    with act.Fori(0, tiles // 2) as i:
                        high(1, slot_uses(l, start) + i)
                        high(0, slot_uses(l, start) + i + 1)

                act.wait_ge(rows_in, (l + 2) * 16)
                act.activation(cond_rows[:], cond_rows[:], ACT.Silu).then_inc(rows_made, 1)
                with act.Fori(0, KT // 2 - 1) as i:
                    for p in range(2):
                        high(p, slot_uses(l, T_OUT) + i + 1)
                high(0, slot_uses(l, T_FF))
                norm(1)
                for chunk, (n, start) in enumerate(zip(FF_CHUNKS, FF_START)):
                    with act.Fori(0, n) as j:
                        high(1, slot_uses(l, start) + j)
                        act.wait_ge(tile_done[0], 1 + slot_uses(l, start) + j + 1)
                        act.activation(two(tmp[:, 0, 0:T]), acc_all(0), ACT.Silu).then_inc(acc_free[0], 1)
                        high(0, slot_uses(l, start) + j + 1)
                        act.wait_ge(acc_free[1], 1 + acc_uses(l, start + 1) + j + 1)
                        act.activation(y_hi[:, bass.ds(j, 1), :].rearrange("p a n -> p (a n)"), tmp[:, 1, 0:T],
                                       ACT.Copy).then_inc(hid_hi, 1)
                    if chunk < len(FF_CHUNKS) - 1:
                        high_pairs(start + 2 * n, KT)
                    else:
                        with act.Fori(0, KT // 2 - 1) as i:
                            high(1, slot_uses(l, start + 2 * n) + i)
                            high(0, slot_uses(l, start + 2 * n) + i + 1)
                        high(1, slot_uses(l, start + 2 * n) + KT // 2 - 1)
                assert steps.n == ACT_STEPS, steps.n

        @block.vector
        def _(dve):
            dve.memset(mean[:], 0.0).then_inc(dve_step, 1)
            dve.wait_ge(dve_step, 1)
            dve.wait_ge(rows_made, 1)
            for n in range(NROWS):
                dve.wait_ge(ada_in[n % ROW_SLOTS], 16 * (n // ROW_SLOTS + 1))
                for s in range(2):
                    if n or s:
                        dve.wait_ge(mod_used, 2 * n + s)
                    dve.scalar_tensor_tensor(out=products, in0=ada[n % ROW_SLOTS][:], scalar=1.0,
                                             in1=cond_rows[:, s, :], op0=ALU.mult, op1=ALU.mult,
                                             accum_out=mods_next[:, n, s:s + 1]).then_inc(mod_used, 1)
            dve.wait_ge(mod_used, 2 * NROWS)
            dve.wait_ge(par_in, 16 * NPAR)
            dve.tensor_tensor(mods_next[:, 0:NROWS, :], mods_next[:, 0:NROWS, :], wide(b_ada[:, 0:NROWS], 2), ALU.add)
            dve.wait_ge(ada_cols_used, NMID - NROWS)
            dve.tensor_tensor(mods_next[:, NROWS:NMID, :], acc[0][:, 0, 0:2 * (NMID - NROWS)].rearrange("p (m s) -> p m s", s=2),
                              wide(b_ada[:, NROWS:NMID], 2), ALU.add).then_inc(dve_step, 1)
            dve.wait_ge(dve_step, 2)
            dve.wait_ge(x_in, 16)

            with dve.Fori(0, DEPTH) as l:
                steps = Count(DVE_STEPS)

                def link(ins):
                    ins.then_inc(dve_step, 1)
                    dve.wait_ge(dve_step, steps.up(l) + 2)

                def take(b, name):
                    dve.wait_ge(full[b], after(b, name, l))

                def newton(name):
                    dve.wait_ge(root_made, l * NR + ROOTS.index(name) + 1)
                    link(dve.tensor_tensor(rstd[:], root[:], root[:], ALU.mult))
                    link(dve.scalar_tensor_tensor(out=rstd[:], in0=rstd[:], scalar=-0.5, in1=mean[:, 0:T],
                                                  op0=ALU.mult, op1=ALU.mult))
                    return dve.scalar_tensor_tensor(out=rstd[:], in0=rstd[:], scalar=1.5, in1=root[:],
                                                    op0=ALU.add, op1=ALU.mult)

                def mean_from(b, name, half, width):
                    take(b, name)
                    dve.tensor_scalar(mean[:, halves[half]], bank[b][:, 0:HALF], 1.0 / width, EPS,
                                      ALU.mult, ALU.add).then_inc(free[b], 1)

                def norm(w):
                    name = ("n1", "n2")[w]
                    shift = (SHIFT1, SHIFT2)[w]
                    mean_from("S", name, 0, D)
                    mean_from("P", name, 1, D)
                    link(newton(name))

                    def scale(k):
                        for s, cols in STREAMS:
                            ins = dve.scalar_tensor_tensor(out=tmp[:, k % 2, cols], in0=x[:, k, cols],
                                                           scalar=gain[:, w, k, s:s + 1], in1=rstd[:, cols],
                                                           op0=ALU.mult, op1=ALU.mult)
                        ins.then_inc(scaled, 1)

                    scale(0)
                    for k in range(KT):
                        if k + 1 < KT:
                            if k:
                                dve.wait_ge(h_made, l * 16 + w * 8 + k)
                            scale(k + 1)
                        dve.wait_ge(h_hi_made, l * 16 + w * 8 + k + 1)
                        for s, cols in STREAMS:
                            ins = dve.scalar_tensor_tensor(out=h_lo[:, k, cols], in0=tmp[:, k % 2, cols],
                                                           scalar=mods[:, shift + k, s:s + 1],
                                                           in1=h_hi[:, k, cols].bitcast(F32),
                                                           op0=ALU.add, op1=ALU.subtract)
                        ins.then_inc(h_made, 1)

                dve.wait_ge(acc_free[0], 1 + l * (WN - 1))
                dve.wait_ge(acc_free[1], 1 + l * WN)
                dve.tensor_copy(small[:], small_all[:, bass.ds(l, 1), :].rearrange("p a n -> p (a n)"))
                dve.tensor_copy(b_turn[:], b_ada[:, NMID:NMID + DEPTH * NMOD].rearrange("p (l m) -> p l m", l=DEPTH)[
                    :, bass.ds(l, 1), :].rearrange("p a m -> p (a m)"))
                link(dve.tensor_copy(mods[:, 0:NMID, :], mods_next[:]))

                def gains(w, sc, g):
                    return dve.scalar_tensor_tensor(out=gain[:, w], in0=mods[:, sc:sc + KT, :], scalar=1.0,
                                                    in1=wide(small[:, g:g + KT], 2), op0=ALU.add, op1=ALU.mult)

                gains(0, SCALE1, C_G1)
                link(dve.tensor_scalar(small[:, C_QG:C_QG + 1], small[:, C_QG:C_QG + 1], 64 ** -0.5, None, ALU.mult))

                norm(0)
                dve.wait_ge(tile_done[1], 1 + slot_uses(l, 1) + 1)
                dve.tensor_copy(two(lrT[:]), acc[1][0:LRW, :, 0:HALF]).then_inc(acc_free[1], 1)
                for d, (b0, b1, name, col) in enumerate((("S", "P", "zf", C_BF), ("O", "X", "zb", C_BB))):
                    for half, b in enumerate((b0, b1)):
                        take(b, name)
                        dve.tensor_scalar(z[:, d, halves[half]], bank[b][:, 0:HALF], small[:, col:col + 1], None,
                                          ALU.add).then_inc(free[b], 1)

                def rotate(i, t, b0, b1, name, dst):
                    dve.wait_ge(acc_free[t % 2], 1 + acc_uses(l, t) + 1)
                    dve.tensor_tensor(tmp[:, 0, 0:T], kq[:, i, :], rope[:, 0, :], ALU.mult)
                    for half, b in enumerate((b0, b1)):
                        take(b, name)
                        dve.tensor_tensor(tmp[:, 1, halves[half]], bank[b][:, 0:HALF], rope[:, 1, halves[half]],
                                          ALU.mult).then_inc(free[b], 1)
                    dve.wait_ge(free[b1], 1 + after(b1, name, l))
                    return dve.tensor_tensor(dst[:], tmp[:, 0, 0:T], tmp[:, 1, 0:T], ALU.add)

                link(rotate(0, T_K, "S", "P", "rk", kr))
                link(dve.memset(root[:], 1.0))
                link(dve.memset(root[:, 0:T:CHUNK], 0.0))
                for d in range(2):
                    dve.wait_ge(log_made, l * 2 + d + 1)
                    link(dve.scalar_tensor_tensor(out=z[:, d, :], in0=z[:, d, :], scalar=0.0, in1=zl[:, d, :],
                                                  op0=ALU.min, op1=ALU.subtract))
                    turn = slice(None, None, -1) if d else slice(None)
                    link(dve.tensor_tensor_scan(bcum[:, d, turn], root[:], z[:, d, turn], 0.0, ALU.mult, ALU.add))
                for b, n, cols in (("S", 4, slice(0, 4)), ("P", 1, slice(4, 5))):
                    take(b, "va0")
                    dve.tensor_copy(v_la[:, cols, 0:P], bank[b][:, 0:n * P].rearrange("p (n f) -> p n f", f=P)
                                    ).then_inc(free[b], 1)
                for d in range(2):
                    end = (CHUNK - 1, 0)[d]
                    sub = bcum[:, d, :].rearrange("p (n s) -> p n s", s=SUB)
                    whole = bcum[:, d, :].rearrange("p (n s) -> p n s", s=CHUNK)
                    link(dve.tensor_tensor(z[:, d, :].rearrange("p (n s) -> p n s", s=SUB), sub,
                                           wide(bcum[:, d, SUB // 2:T:SUB], SUB), ALU.subtract))
                    dve.tensor_scalar(z[:, d, :], z[:, d, :], LIMIT * TAU, None, ALU.min)
                    dve.tensor_tensor(zl[:, d, :].rearrange("p (n s) -> p n s", s=CHUNK),
                                      wide(bcum[:, d, end:T:CHUNK], CHUNK), whole, ALU.subtract).then_inc(args_made, 1)
                rotate(1, T_Q, "O", "X", "rq", qr).then_inc(rope_made, 1)
                dve.wait_ge(rope_made, l + 1)
                for b, n, cols in (("O", 4, slice(0, 4)), ("X", 1, slice(4, 5))):
                    take(b, "va1")
                    dve.tensor_copy(v_la[:, cols, P:2 * P], bank[b][:, 0:n * P].rearrange("p (n f) -> p n f", f=P)
                                    ).then_inc(free[b], 1)
                for i, (buf, fac, made) in enumerate(((zl, kr, kd_made), (z, qr, qe_made), (None, None, None), (kq, qr, qi_made))):
                    for d in range(2):
                        if buf is None:
                            continue
                        dve.wait_ge(exps_made, l * 8 + 2 * i + d + 1)
                        dve.tensor_tensor(buf[:, d, :], buf[:, d, :], fac[:], ALU.mult).then_inc(made, 1)
                take("S", "kdf")
                dve.tensor_copy(kdT[:, 0, 0:4, :], S[:].rearrange("p (n f) -> p n f", f=P)).then_inc(free["S"], 1)
                take("P", "kdp")
                dve.tensor_copy(kdT[:, :, 4, :], PT[:, 0:2 * P].rearrange("p (d f) -> p d f", f=P)).then_inc(free["P"], 1)
                take("O", "kdb")
                dve.tensor_copy(kdT[:, 1, 0:4, :], O[:].rearrange("p (n f) -> p n f", f=P)).then_inc(free["O"], 1)
                dve.tensor_copy(states[:, 0, 0, :], state_in[:, bass.ds(l, 1), 0, :].rearrange("p a n -> p (a n)"))
                dve.tensor_copy(states[:, 1, 7, :], state_in[:, bass.ds(l, 1), 1, :].rearrange("p a n -> p (a n)"))
                dve.memset(states[:, 0, 8, :], 0.0)
                dve.memset(states[:, 1, 9, :], 0.0)
                for b, name in (("S", "ufa"), ("P", "ufb"), ("O", "uba"), ("X", "ubb")):
                    take(b, name)

                def added(d, n):
                    return (("S", "P"), ("O", "X"))[d][n % 2], slice(n // 2 * CHUNK, n // 2 * CHUNK + CHUNK)

                def scan(d, n, dst):
                    b, cols = added(d, n)
                    return dve.scalar_tensor_tensor(out=dst, in0=states[:, d, n, :], scalar=decay[:, d, n:n + 1],
                                                    in1=bank[b][:, cols], op0=ALU.mult, op1=ALU.add)

                dve.wait_ge(s_out, 1 + 16 * l)
                for d, n in ((0, 8), (1, 9)):
                    b, cols = added(d, n)
                    link(dve.tensor_copy(states[:, d, 17 - n, :], bank[b][:, cols]))
                scan(0, 9, final[:, 0, :])
                scan(1, 8, final[:, 1, :])
                for i in range(7):
                    f = scan(0, i, states[:, 0, i + 1, :])
                    if i < 5:
                        f.then_inc(dve_step, 1)
                        nf = steps.up(l) + 2
                    else:
                        f.then_inc(free["PS"[i - 5]], 1)
                    r = scan(1, 7 - i, states[:, 1, 6 - i, :])
                    if i < 5:
                        r.then_inc(dve_step, 1)
                        nf = steps.up(l) + 2
                        dve.wait_ge(dve_step, nf)
                    else:
                        r.then_inc(free["OX"[i - 5]], 1)
                        dve.wait_ge(free["PS"[i - 5]], 1 + after("PS"[i - 5], ("ufb", "ufa")[i - 5], l))
                        dve.wait_ge(free["OX"[i - 5]], 1 + after("OX"[i - 5], ("uba", "ubb")[i - 5], l))

                def kk_args(j):
                    for d in range(2):
                        b = bcum[:, d, j * P:(j + 1) * P]
                        ref = b[:, SUB // 2:P:SUB].rearrange("p (c i) -> p c i", c=2)
                        for ch in range(2):
                            ins = dve.tensor_tensor(
                                kk[:, j % 2, d, ch], wide(ref[:, ch, :], CHUNK),
                                b[:, ch * CHUNK:(ch + 1) * CHUNK].unsqueeze(1).broadcast_to([P, 4, CHUNK]), ALU.subtract)
                    link(ins)
                    dve.tensor_scalar(kk[:, j % 2], kk[:, j % 2], LIMIT * TAU, None, ALU.min).then_inc(kk_arg, 1)

                def kk_mul(j):
                    dve.wait_ge(kk_exp, l * NP + j + 1)
                    kj = kr[:, j * P:(j + 1) * P]
                    for d in range(2):
                        for ch in range(2):
                            ins = dve.tensor_tensor(
                                kk[:, j % 2, d, ch], kk[:, j % 2, d, ch],
                                kj[:, ch * CHUNK:(ch + 1) * CHUNK].unsqueeze(1).broadcast_to([P, 4, CHUNK]), ALU.mult)
                    ins.then_inc(kk_made, 1)

                def gla_mask(j):
                    take("S", ("sc", j))
                    dve.tensor_tensor(tmp[:, j % 2, 0:512], S[:], causal[:], ALU.mult).then_inc(free["S"], 1)
                    dve.wait_ge(free["S"], 1 + after("S", ("sc", j), l))
                    dve.tensor_tensor(att[:, j % 2, :], tmp[:, j % 2, 0:256], tmp[:, j % 2, 256:512],
                                      ALU.add).then_inc(att_made, 1)

                def gla_take(j):
                    for ch, b in enumerate("OX"):
                        take(b, ("go", j))
                        dve.tensor_copy(gla_o[:, :, j * P + ch * CHUNK:j * P + (ch + 1) * CHUNK],
                                        bank[b][:, 0:P].rearrange("p (h n) -> p h n", h=2)).then_inc(free[b], 1)

                def square_mean(name):
                    mean_from("X", name, name[2], CHUNK)

                def finish_norm(kind, c):
                    link(newton((kind, c)))
                    dst, col = {"q": (qn, C_QG), "k": (kn, C_KG), "g": (gla_o, C_LG)}[kind]
                    row = dst[:, c if kind == "g" else c % 2, :]
                    dve.scalar_tensor_tensor(out=row, in0=row, scalar=small[:, col:col + 1], in1=rstd[:],
                                             op0=ALU.mult, op1=ALU.mult).then_inc(norm_done, 1)

                def to_pool(i):
                    t = T_POOL + i
                    dve.wait_ge(tile_done[t % 2], 1 + slot_uses(l, t) + 1)
                    u, s0, s1 = mean, tmp[:, 0, :], tmp[:, 1, :]
                    dve.memset(mean[:, 0:LAT0], 0.0)
                    dve.memset(mean[:, LAT0 + LAT:CTX0], 0.0)
                    dve.memset(mean[:, CTX0 + CTX:PADT], 0.0)
                    dve.tensor_copy(mean[:, LAT0:LAT0 + HALF], acc[t % 2][:, 0, 0:HALF])
                    dve.tensor_copy(mean[:, LAT0 + HALF:LAT0 + LAT], acc[t % 2][:, 1, 0:LAT - HALF])
                    dve.tensor_copy(mean[:, CTX0:CTX0 + CTX], acc[t % 2][:, 1, LAT - HALF:HALF]).then_inc(acc_free[t % 2], 1)
                    dve.wait_ge(acc_free[t % 2], 1 + acc_uses(l, t) + 1)
                    src, reach = mean[:], 1
                    link(dve.tensor_tensor(s0[:, 1:PADT], mean[:, 0:PADT - 1], mean[:, 1:PADT], ALU.add))
                    bufs, lo = (s0, s1), 1
                    for k in range(1, 2 + 2 * i):
                        a_, b_ = bufs[(k - 1) % 2], bufs[k % 2]
                        r = 2 ** (k - 1)
                        n0, n1 = lo + r, PADT - lo - r + 1
                        n1 = PADT - (2 ** k - 1)
                        link(dve.tensor_tensor(b_[:, n0:n1], a_[:, n0 - r:n1 - r], a_[:, n0 + r:n1 + r], ALU.add))
                        lo = n0
                    for rows, src in ((slice(0, 64), s0), (slice(64, P), s1)):
                        for s, (first, last) in enumerate(((LAT0, LAT0 + LAT - 8), (CTX0, CTX0 + CTX - 8))):
                            for e, at in enumerate((first, last)):
                                ins = dve.tensor_tensor(src[rows, at:at + 8], src[rows, at:at + 8],
                                                        edges[rows, i, s, e, :], ALU.mult)
                    link(ins)
                    for rows, src in ((slice(0, 64), s0), (slice(64, P), s1)):
                        for first, cols in ((LAT0, slice(0, LAT)), (CTX0, slice(LAT, T))):
                            n = cols.stop - cols.start
                            ins = dve.scalar_tensor_tensor(out=root[rows, cols], in0=src[rows, first:first + n],
                                                           scalar=inv_w[rows, i:i + 1], in1=mean[rows, first:first + n],
                                                           op0=ALU.mult, op1=ALU.subtract)
                    ins.then_inc(pool_d, 1)

                kk_args(0)
                for g in range(STEPS + 1):
                    for name in x_fills_at(g - 2):
                        if name[0] in ("qsum", "ksum", "gsum") and name[2]:
                            finish_norm(name[0][0], name[1])
                    for j in range(NP):
                        if g == 4 + j:
                            kk_mul(j)
                    for j in range(NP):
                        if g == 5 + j:
                            gla_mask(j)
                        if g == 6 + j:
                            gla_take(j)
                        if j and g == 3 + j:
                            pass
                    for j in range(1, NP):
                        if g == 3 + j:
                            kk_args(j)
                    for c, u in units_at(g, 1):
                        dve.wait_ge(scores_made, l * NU + c * UNITS + u + 1)
                        e, b = u // 5, u % 5
                        w = 384 if b < CTX_UNIT else P
                        if b == 0:
                            dve.wait_ge(bias_in[e], 16 * (l * PAIRS + c + 1))
                        dve.wait_ge(prob_made, 1 + l * NU + c * UNITS + u)
                        added_ = bias[e][:, BIAS_KIND[b], :] if b < CTX_UNIT else bias[e][:, 0, 256:384]
                        if units_at(g, 3):
                            (_, v), = units_at(g, 3)
                            dve.reciprocal(row_stat[:, 2, v % 4:v % 4 + 1], row_stat[:, 1, v % 4:v % 4 + 1]
                                           ).then_inc(dve_step, 1)
                            reciprocal_made = steps.up(l) + 2
                        else:
                            dve.memset(row_stat[:, 2, 2 + u % 2:3 + u % 2], 0.0)
                        dve.tensor_tensor_reduce(neg_s[:, 0:w], S[:, 0:w], added_, -1.0, 3e38, ALU.add, ALU.min,
                                                 row_stat[:, 0, u % 4:u % 4 + 1]).then_inc(biased, 1)
                    for c, u in units_at(g, 3):
                        e, b = u // 5, u % 5
                        if units_at(g, 1):
                            dve.wait_ge(dve_step, reciprocal_made)
                        else:
                            dve.wait_ge(prob_made, 1 + l * NU + c * UNITS + u + 1)
                            link(dve.reciprocal(row_stat[:, 2, u % 4:u % 4 + 1], row_stat[:, 1, u % 4:u % 4 + 1]))
                        take("O", ("pv", c, u))
                        dve.tensor_scalar(o_tok[:, b, 64 * e:64 * e + 64], O[:, 0:64], row_stat[:, 2, u % 4:u % 4 + 1],
                                          None, ALU.mult).then_inc(free["O"], 1)
                    for name in x_fills_at(g - 1):
                        if name[0] in ("qsum", "ksum", "gsum"):
                            square_mean(name)
                        if name[0] == "vtr":
                            take("X", name)
                            c, i = name[1:]
                            dve.tensor_copy(v_tok[c % 2][:, 4 * i:4 * i + 4, :], X[:].rearrange("p (n f) -> p n f", f=P)
                                            ).then_inc(free["X"], 1)
                        if name[0] == "oT":
                            take("X", name)
                            c, b = name[1:]
                            if b < CTX_UNIT:
                                hi_, lo_ = grid(y_hi[:, 2 + c, :], 16 * b, 16), grid(y_lo[:, 2 + c, :], 16 * b, 16)
                                src = X[:, 0:P].rearrange("p (w r) -> p r w", r=GR)
                            else:
                                hi_, lo_, src = y_hi[:, 2 + c, LAT:T], y_lo[:, 2 + c, LAT:T], X[:, 0:P]
                            link(dve.tensor_copy(hi_, src))
                            dve.tensor_tensor(lo_, src, hi_.bitcast(F32), ALU.subtract).then_inc(free["X"], 1)
                        if name[0] == "pool":
                            take("X", name)
                            i, half = name[1:]
                            hi_, lo_ = y_hi[:, i, halves[half]], y_lo[:, i, halves[half]]
                            link(dve.tensor_scalar(hi_, X[:, 0:HALF], small[:, C_PS + i:C_PS + i + 1], None, ALU.mult))
                            dve.scalar_tensor_tensor(out=lo_, in0=X[:, 0:HALF], scalar=small[:, C_PS + i:C_PS + i + 1],
                                                     in1=hi_.bitcast(F32), op0=ALU.mult, op1=ALU.subtract
                                                     ).then_inc(free["X"], 1)
                    for i in range(2):
                        if g == 45 + 3 * i:
                            dve.wait_ge(gate_exp, l * 2 + i + 1)
                            link(dve.tensor_scalar(tmp[:, i, 0:T], tmp[:, i, 0:T], 1.0, None, ALU.add))
                            link(dve.reciprocal(tmp[:, i, 0:T], tmp[:, i, 0:T]))
                            link(dve.tensor_tensor(gate[:, i, :], gate[:, i, :], tmp[:, i, 0:T], ALU.mult))
                            dve.tensor_tensor(gla_o[:, i, :], gla_o[:, i, :], gate[:, i, :], ALU.mult).then_inc(gated, 1)
                    for i in range(2):
                        if g == 51 + i:
                            dve.wait_ge(gated_hi, l * 2 + i + 1)
                            link(dve.tensor_tensor(y_lo[:, 6 + i, :], gla_o[:, i, :], y_hi[:, 6 + i, :].bitcast(F32),
                                                   ALU.subtract))
                    for i in range(2):
                        if g == 51 + 3 * i:
                            to_pool(i)

                def update(p, m, gates, done, in_loop=True):
                    dve.wait_ge(tile_done[p], 1 + done)
                    for n, (s, half, first, last) in enumerate(PIECES):
                        xs = x[:, bass.ds(m, 1), half * HALF + first:half * HALF + last].rearrange("p a n -> p (a n)")
                        ins = dve.scalar_tensor_tensor(
                            out=xs, in0=acc[p][:, half, first:last],
                            scalar=mods[:, bass.ds(gates + m, 1), s:s + 1].rearrange("p a s -> p (a s)"), in1=xs,
                            op0=ALU.mult, op1=ALU.add)
                    ins.then_inc(acc_free[p], 1)

                def add_bias(k, dst, n):
                    dve.wait_ge(mod_used, 2 * (l * NMOD + NROWS + k))
                    return dve.tensor_tensor(dst, dst, wide(b_turn[:, k - n:k], 2), ALU.add)

                def updates(start, gates, mods_of=None, gates_made=None):
                    with dve.Fori(0, KT // 2) as i:
                        if gates_made is not None:
                            dve.wait_ge(dve_step, gates_made)
                        for p in range(2):
                            dve.wait_ge(acc_free[p], 1 + acc_uses(l, start + p) + i)
                            update(p, 2 * i + p, gates, slot_uses(l, start) + i + 1)
                            if mods_of:
                                mods_of(i, p)

                def mods_in_pairs(first, dst, m):
                    def of(i, p):
                        dve.wait_ge(mod_in[p], 16 * (l * (NMOD // 2) + first // 2 + i + 1))
                        products_of(p, first + 2 * i + p, dst, m + 2 * i + p)
                    return of

                def products_of(p, k, dst, m):
                    for s in range(2):
                        dve.wait_ge(mod_used, 2 * (l * NMOD + NROWS + k) + s)
                        dve.scalar_tensor_tensor(
                            out=products, in0=mod_w[p][:], scalar=1.0, in1=cond_rows[:, s, :], op0=ALU.mult, op1=ALU.mult,
                            accum_out=dst[:, bass.ds(m, 1), s:s + 1].rearrange("p a s -> p (a s)")).then_inc(mod_used, 1)

                def mods_by_two(i, p):
                    dve.wait_ge(rows_made, l + 2)
                    for q in range(2):
                        dve.wait_ge(mod_in[q], 16 * (l * (NMOD // 2) + 2 * i + p + 1))
                        products_of(q, 4 * i + 2 * p + q, mods, SHIFT2 + 4 * i + 2 * p + q)

                updates(T_OUT, GATE1, mods_by_two)
                k = 2 * KT
                link(add_bias(k, mods[:, SHIFT2:SHIFT2 + 2 * KT, :], 2 * KT))
                link(gains(1, SCALE2, C_G2))
                norm(1)
                made = 0
                for chunk, (n, start) in enumerate(zip(FF_CHUNKS, FF_START)):
                    mods_of = (mods_in_pairs(k, mods, GATE2), mods_in_pairs(k, mods_next, KT), None)[chunk]
                    with dve.Fori(0, n // 2) as i:
                        for p in range(2):
                            j = 2 * i + p
                            if mods_of:
                                mods_of(i, p)
                            dve.wait_ge(tile_done[1], 1 + slot_uses(l, start) + j + 1)
                            dve.wait_ge(acc_free[0], 1 + acc_uses(l, start) + j + 1)
                            dve.wait_ge(hid_lo, 1 + l * NHID + made + j)
                            dve.tensor_tensor(two(tmp[:, 1, 0:T]), two(tmp[:, 0, 0:T]), acc_all(1), ALU.mult
                                              ).then_inc(acc_free[1], 1)
                            dve.wait_ge(hid_hi, l * NHID + made + j + 1)
                            dve.tensor_tensor(y_lo[:, bass.ds(j, 1), :].rearrange("p a n -> p (a n)"), tmp[:, 1, 0:T],
                                              y_hi[:, bass.ds(j, 1), :].rearrange("p a n -> p (a n)").bitcast(F32),
                                              ALU.subtract).then_inc(hid_lo, 1)
                    made += n
                    if chunk < 2:
                        k += n
                        if chunk == 0:
                            add_bias(k, mods[:, GATE2:GATE2 + KT, :], KT).then_inc(dve_step, 1)
                            gates_made = steps.up(l) + 2
                        updates(start + 2 * n, GATE2, mods_in_pairs(k, mods_next, (0, GATE1)[chunk]), gates_made)
                        k += KT
                    else:
                        updates(start + 2 * n, GATE2)
                assert k == NMOD
                link(add_bias(k, mods_next[:], NMID))
                assert steps.n == DVE_STEPS, steps.n

        @block.tensor
        def _(pe):
            pe.wait_ge(cond_made, 1)
            for n in range(NMID - NROWS):
                slot = ROW_SLOTS + n % COL_SLOTS
                pe.wait_ge(ada_in[slot], (n // COL_SLOTS + 1) * 16)
                for k in range(KT):
                    mm = pe.matmul(acc[0][:, 0, 2 * n:2 * n + 2], ada[slot][:, k * P:(k + 1) * P], cond[:, k, :],
                                   start=k == 0, stop=k == KT - 1)
                mm.then_inc(ada_cols_used, 1)
            pe.wait_ge(par_in, 16 * NPAR)

            with pe.Fori(0, DEPTH) as l:
                def claim(b, name):
                    pe.wait_ge(free[b], 1 + before(b, name, l))

                def gemm(p, hi, lo, first=0, last=MMS, kts=KT, slot=None, wait_h=False, start=True, stop=True):
                    slot = p if slot is None else slot
                    for n in range(first, min(last, 6 * kts)):
                        k, j = divmod(n, 6)
                        if wait_h and j == 0:
                            pe.wait_ge(h_made, wait_h(k))
                        w = (w_hi, w_hi, w_lo)[j // 2][p]
                        m = (hi, lo, hi)[j // 2]
                        mm = pe.matmul(acc[slot][:, j % 2, 0:HALF], w[:, k % KT * P:(k % KT + 1) * P] if kts <= KT else None,
                                       m(k, j % 2), start=start and n < 2, stop=stop and n >= 6 * kts - 2)
                        if n == 6 * kts - 1:
                            mm.then_inc(tile_done[p], 1)

                def h(part, base=0):
                    return lambda k, half: part[:, base + k, halves[half]]

                def ready(t):
                    pe.wait_ge(lo_made[t % 2], 1 + slot_uses(l, t) + 1)
                    pe.wait_ge(acc_free[t % 2], 1 + acc_uses(l, t))

                def norm(w):
                    name = ("n1", "n2")[w]
                    claim("S", name)
                    claim("P", name)
                    if w:
                        pe.wait_ge(pt_free, 1 + (l + 1) * NU)
                        pe.wait_ge(biased, 1 + (l + 1) * NU)
                    for k in range(KT):
                        pe.wait_ge(norm_sq, l * 16 + w * 8 + k + 1)
                        for half, b in enumerate("SP"):
                            mm = pe.matmul(bank[b][:, 0:HALF], ones, tmp[:, k % 2, halves[half]], start=k == 0, stop=k == KT - 1)
                            if k == KT - 1:
                                mm.then_inc(full[b], 1)
                        if k < KT - 1:
                            mm.then_inc(sq_used, 1)

                def both_halves(b0, b1, name, lhsT, row):
                    for half, b in enumerate((b0, b1)):
                        claim(b, name)
                        pe.matmul(bank[b][:, 0:HALF], lhsT, row[:, halves[half]], start=True, stop=True).then_inc(full[b], 1)

                def transposes(b, name, tiles):
                    claim(b, name)
                    for n, src in enumerate(tiles):
                        mm = pe.transpose(bank[b][:, n * P:(n + 1) * P], src, ident)
                    mm.then_inc(full[b], 1)

                norm(0)
                pe.wait_ge(lo_made[0], 1 + slot_uses(l, 0) + 1)
                pe.wait_ge(acc_free[1], 1 + acc_uses(l, 1))
                gemm(0, h(h_hi), h(h_lo), kts=KT // 2, slot=1, wait_h=lambda k: l * 16 + k + 1, stop=False)
                pe.wait_ge(lo_made[1], 1 + slot_uses(l, 1) + 1)
                gemm(1, h(h_hi, KT // 2), h(h_lo, KT // 2), kts=KT // 2, wait_h=lambda k: l * 16 + k + 5, start=False)
                ready(T_K)
                gemm(0, h(h_hi), h(h_lo))
                pe.wait_ge(layer_in, (l + 1) * 32)
                pe.wait_ge(acc_free[1], 1 + acc_uses(l, 1) + 1)
                both_halves("S", "P", "zf", wgate[:, 0:P], lrT)
                both_halves("O", "X", "zb", wgate[:, P:2 * P], lrT)
                ready(T_Q)
                gemm(1, h(h_hi), h(h_lo))
                pe.wait_ge(acc_free[T_K % 2], 1 + acc_uses(l, T_K) + 1)
                both_halves("S", "P", "rk", swap, kq[:, 0, :])
                ready(T_V)
                gemm(0, h(h_hi), h(h_lo))
                pe.wait_ge(acc_free[T_Q % 2], 1 + acc_uses(l, T_Q) + 1)
                both_halves("O", "X", "rq", swap, kq[:, 1, :])
                pe.wait_ge(acc_free[T_V % 2], 1 + acc_uses(l, T_V) + 1)
                transposes("S", "va0", [vT[:, n * P:(n + 1) * P] for n in range(4)])
                transposes("P", "va0", [vT[:, 4 * P:5 * P]])
                ready(T_V + 1)
                gemm(1, h(h_hi), h(h_lo))

                def scores(c, u):
                    e, b = u // 5, u % 5
                    rows = slice(64 * e, 64 * e + 64)
                    if u == 0:
                        pe.wait_ge(norm_done, 1 + norms(l, ("k", c)) + 1)
                        pe.wait_ge(ctx_in, (l + 1) * 32)
                    if c == u == 0:
                        claim("S", "n2")
                    pe.wait_ge(biased, 1 + l * NU + c * UNITS + u)
                    if b < CTX_UNIT:
                        q = qn[rows, c % 2, b * P:(b + 1) * P]
                        k0 = KEY_START[b] * GR
                        pe.matmul(S[:, 0:256], q, kn[rows, c % 2, k0:k0 + 256], start=True, stop=True)
                        mm = pe.matmul(S[:, 256:384], q, ctx_k[rows, c, :], start=True, stop=True)
                    else:
                        mm = pe.matmul(S[:, 0:P], qn[rows, c % 2, LAT:T], kn[rows, c % 2, LAT:T], start=True, stop=True)
                    mm.then_inc(scores_made, 1)

                def turn_probs(c, u):
                    n = l * NU + c * UNITS + u
                    pe.wait_ge(prob_made, 1 + n + 1)
                    pe.wait_ge(pt_free, 1 + n)
                    if c == u == 0:
                        claim("P", "n2")
                    pr = prob[:, u % 2, :]
                    for i in range(3 if u % 5 < CTX_UNIT else 1):
                        mm = pe.transpose(PT[:, i * P:(i + 1) * P], pr[:, i * P:(i + 1) * P], ident)
                    mm.then_inc(pt_full, 1)

                def values(c, u):
                    e, b = u // 5, u % 5
                    pe.wait_ge(pt_free, 1 + l * NU + c * UNITS + u + 1)
                    if u == 0:
                        pe.wait_ge(free["X"], 1 + after("X", ("vtr", c, 1), l))
                    claim("O", ("pv", c, u))
                    vt = v_tok[c % 2]
                    if b < CTX_UNIT:
                        for i, grp in enumerate(BLOCK_GROUPS[b]):
                            pe.matmul(O[:, 0:64], probT[:, u % 2, i * P:(i + 1) * P], vt[:, grp, 64 * e:64 * e + 64],
                                      start=i == 0, stop=False)
                        mm = pe.matmul(O[:, 0:64], probT[:, u % 2, 256:384], ctx_v[:, (2 * c + e) * 64:(2 * c + e + 1) * 64],
                                       start=False, stop=True)
                    else:
                        mm = pe.matmul(O[:, 0:64], probT[:, u % 2, 0:P], vt[:, 7, 64 * e:64 * e + 64], start=True, stop=True)
                    mm.then_inc(full["O"], 1)

                def gla_scores(j):
                    pe.wait_ge(kk_made, l * NP + j + 1)
                    pe.wait_ge(qh_made, (l * NP + j + 1) * 2)
                    claim("S", ("sc", j))
                    for d in range(2):
                        for ch in range(2):
                            for i in range(4):
                                t0 = ch * CHUNK + i * SUB
                                mm = pe.matmul(S[ch * CHUNK:(ch + 1) * CHUNK, d * 256 + i * 64:d * 256 + i * 64 + 64],
                                               kk[:, j % 2, d, ch, i, :], q_heads[:, d, :, t0:t0 + SUB],
                                               start=True, stop=True)
                    mm.then_inc(full["S"], 1)

                def gla_outs(j):
                    pe.wait_ge(qi_made, l * 2 + 2)
                    pe.wait_ge(sh_made, (l * NP + j + 1) * 4)
                    pe.wait_ge(att_made, l * NP + j + 1)
                    for ch, b in enumerate("OX"):
                        claim(b, ("go", j))
                        rows = slice(ch * CHUNK, (ch + 1) * CHUNK)
                        toks = slice(j * P + ch * CHUNK, j * P + (ch + 1) * CHUNK)
                        for hp in range(2):
                            region = bank[b][:, hp * CHUNK:(hp + 1) * CHUNK]
                            for d in range(2):
                                pe.matmul(region, s_heads[:, d, ch, hp * P:(hp + 1) * P], kq[:, d, toks],
                                          start=d == 0, stop=False)
                            for e in range(2):
                                hh = 2 * hp + e
                                mm = pe.matmul(
                                    bank[b][64 * e:64 * e + 64, hp * CHUNK:(hp + 1) * CHUNK],
                                    v_la[rows, j, hh * 64:hh * 64 + 64],
                                    att[rows, j % 2, :].rearrange("p (i h t) -> p i h t", i=4, h=4)[:, :, hh, :],
                                    start=False, stop=True)
                        mm.then_inc(full[b], 1)

                for g in range(STEPS):
                    at, end = product_at(g), product_at(g + 1)
                    while at < end:
                        n = at // MMS
                        stop_at = min(end, (n + 1) * MMS)
                        t = T_PAIR + n
                        if at % MMS == 0:
                            ready(t)
                        if g == 3 and stop_at == end:
                            gemm(t % 2, h(h_hi), h(h_lo), at - n * MMS, stop_at - n * MMS - 2)
                            at = stop_at - 2
                            for b, name in (("S", "ufa"), ("P", "ufb"), ("O", "uba"), ("X", "ubb")):
                                claim(b, name)
                        gemm(t % 2, h(h_hi), h(h_lo), at - n * MMS, stop_at - n * MMS)
                        at = stop_at
                    if g == 0:
                        pe.wait_ge(acc_free[(T_V + 1) % 2], 1 + acc_uses(l, T_V + 1) + 1)
                        transposes("O", "va1", [vT[:, n * P:(n + 1) * P] for n in range(4)])
                        transposes("X", "va1", [vT[:, 4 * P:5 * P]])
                    if g == 2:
                        pe.wait_ge(kd_made, l * 2 + 2)
                        transposes("S", "kdf", [zl[:, 0, n * P:(n + 1) * P] for n in range(4)])
                        transposes("P", "kdp", [zl[:, d, 4 * P:5 * P] for d in range(2)])
                        transposes("O", "kdb", [zl[:, 1, n * P:(n + 1) * P] for n in range(4)])
                    if g == 3:
                        for d, ch, b in ((0, 0, "S"), (0, 1, "P"), (1, 0, "O"), (1, 1, "X")):
                            rows = slice(ch * CHUNK, (ch + 1) * CHUNK)
                            for j in range(NP):
                                for hh in range(4):
                                    mm = pe.matmul(bank[b][32 * hh:32 * hh + 32, j * CHUNK:(j + 1) * CHUNK],
                                                   kdT[rows, d, j, 32 * hh:32 * hh + 32],
                                                   v_la[rows, j, hh * 64:hh * 64 + 64], start=True, stop=True,
                                                   tile_position=(ch * CHUNK, 32 * hh))
                            mm.then_inc(full[b], 1)
                    for j in gla_scores_at(g):
                        gla_scores(j)
                    for j in gla_outs_at(g):
                        gla_outs(j)
                    for c, u in units_at(g, 0):
                        scores(c, u)
                    for c, u in units_at(g, 1):
                        turn_probs(c, u)
                    for c, u in units_at(g, 2):
                        values(c, u)
                    for name in x_fills_at(g):
                        kind, i, n = name if len(name) == 3 else (name[0], name[1], 0)
                        if kind == "oT":
                            pe.wait_ge(free["O"], 1 + after("O", ("pv", i, 5 + n), l))
                            transposes("X", name, [o_tok[:, n, :]])
                        if kind == "vtr":
                            tv = T_PAIR + 3 * i + 2
                            pe.wait_ge(acc_free[tv % 2], 1 + acc_uses(l, tv) + 1)
                            src = [vT[:, col * GR:col * GR + P] for col in V_GROUPS] + [vT[:, LAT:T]]
                            transposes("X", name, src[4 * n:4 * n + 4])
                        if kind in ("qsum", "ksum", "gsum"):
                            if kind == "gsum":
                                pe.wait_ge(gla_sq, l * 2 + i + 1)
                            else:
                                t = T_PAIR + 3 * i + (kind == "ksum")
                                pe.wait_ge(acc_free[t % 2], 1 + acc_uses(l, t) + 1)
                            claim("X", name)
                            pe.matmul(X[:, 0:HALF], blocks, root[:, halves[n]], start=True, stop=True).then_inc(full["X"], 1)
                        if kind == "pool":
                            pe.wait_ge(pool_d, l * 2 + i + 1)
                            claim("X", name)
                            pe.matmul(X[:, 0:HALF], wpool[:, i, :], root[:, halves[n]], start=True, stop=True
                                      ).then_inc(full["X"], 1)

                def stage(start, tiles, hi, lo, kts=KT, wait_h=None, inputs=None):
                    with pe.Fori(0, tiles // 2) as i:
                        if inputs:
                            pe.wait_ge(inputs[0], 1 + inputs[1])
                        for p in range(2):
                            pe.wait_ge(lo_made[p], 1 + slot_uses(l, start) + i + 1)
                            pe.wait_ge(acc_free[p], 1 + acc_uses(l, start + p) + i)
                            gemm(p, h(hi), h(lo), kts=kts, wait_h=wait_h)

                stage(T_OUT, KT, y_hi, y_lo, inputs=(free["X"], (l + 1) * len(FILLS["X"])))
                norm(1)
                made = 0
                for chunk, (n, start) in enumerate(zip(FF_CHUNKS, FF_START)):
                    stage(start, 2 * n, h_hi, h_lo, wait_h=None if chunk else lambda k: l * 16 + 8 + k + 1)
                    made += n
                    stage(start + 2 * n, KT, y_hi, y_lo, kts=n, inputs=(hid_lo, l * NHID + made))


def layout(i):
    import numpy as np

    f = np.float32
    a = {}

    def tiles(w):
        k, m = w.shape
        return w.reshape(k // P, P, m // P, P).transpose(2, 1, 0, 3).reshape(m // P, P, k)

    xs = np.concatenate([i["x_sample"][0], i["x_prompt"][0]], 0)
    a["x"] = xs.T.reshape(KT, P, T).transpose(1, 0, 2)
    a["cond"] = np.stack([i["c"][0], i["c_ctx"]], 1).reshape(KT, P, 2).transpose(1, 0, 2)
    a["cond_rows"] = np.stack([np.stack([i["c"][0], i["c_ctx"]])] * P)
    w_ada = np.zeros((NMID + DEPTH * NMOD, P, D), f)
    w_ada[:DEPTH * NMOD] = i["w_ada"].transpose(0, 2, 1).reshape(DEPTH * NMOD, P, D)
    w_ada[NROWS:NMID] = tiles(i["w_ada"][0][:, NROWS * P:NMID * P])
    a["w_ada"] = w_ada
    a["b_ada"] = np.concatenate([i["b_ada"].reshape(DEPTH * NMOD, P), np.zeros((NMID, P), f)]).T
    w = np.zeros((DEPTH * NT, P, KT * P), f)
    cuts = np.cumsum([256, 512, 512, 512, 128, 128, 256, 256, 16])
    for l in range(DEPTH):
        pool, q, k, v, ql, kl, vl, g, lf, lb = np.split(i["w_in"][l], cuts, 1)
        lr = np.concatenate([lf, lb, np.zeros((D, P - LRW), f)], 1)
        t = w[l * NT:(l + 1) * NT]
        t[0, :, :KT // 2 * P] = tiles(lr[:D // 2])[0]
        t[1, :, :KT // 2 * P] = tiles(lr[D // 2:])[0]
        t[T_K], t[T_Q] = tiles(kl)[0], tiles(ql)[0]
        t[T_V:T_V + 2] = tiles(vl)
        for s, m in enumerate((q, k, v)):
            t[T_PAIR + s:T_G:3] = tiles(m)
        t[T_G:T_POOL] = tiles(g)
        t[T_POOL:T_OUT] = tiles(pool)
        t[T_OUT:T_FF] = tiles(i["w_out"][l])
        win, wout = tiles(i["w_ffn_in"][l]), i["w_ffn_out"][l]
        at, done = T_FF, 0
        for n in FF_CHUNKS:
            t[at:at + 2 * n:2] = win[done:done + n]
            t[at + 1:at + 2 * n:2] = win[NHID + done:NHID + done + n]
            t[at + 2 * n:at + 2 * n + KT, :, :n * P] = tiles(wout[done * P:(done + n) * P])
            at, done = at + 2 * n + KT, done + n
    a["w"] = w
    twice = lambda v: np.concatenate([v, v])
    cols = np.zeros((DEPTH, NSMALL, P), f)
    for l in range(DEPTH):
        cols[l, C_G1:C_G1 + KT] = i["norm1_gain"][l].reshape(KT, P)
        cols[l, C_G2:C_G2 + KT] = i["norm2_gain"][l].reshape(KT, P)
        cols[l, C_PS:C_PS + 2] = i["pool_scale"][l].reshape(2, P)
        cols[l, C_QG], cols[l, C_KG] = twice(i["q_norm_gain"][l]), twice(i["k_norm_gain"][l])
        cols[l, C_BF], cols[l, C_BB] = i["b_gate_f"][l], i["b_gate_b"][l]
        cols[l, C_LG] = twice(i["gla_norm_gain"][l])
    a["small"] = cols.transpose(2, 0, 1)
    wg = np.zeros((DEPTH, LRW, 2 * P), f)
    wg[:, :16, :P], wg[:, 16:, P:] = i["w_gate_f"], i["w_gate_b"]
    a["wgate"] = wg
    wp = np.zeros((DEPTH, P, 2, P), f)
    for g in range(4):
        r = slice(g % 2 * 64, g % 2 * 64 + 64)
        wp[:, r, g // 2, r] = i["w_pool"][:, g]
    a["wpool"] = wp
    a["state"] = np.stack([i["state_gla_fwd"][0], i["state_gla_bwd"][0]], 1).reshape(DEPTH, 2, P, CHUNK).transpose(2, 0, 1, 3)
    a["ctx_k"] = i["cache_na_k"][0].reshape(DEPTH, PAIRS, 2, P, 64).transpose(0, 2, 4, 1, 3).reshape(DEPTH, P, PAIRS, P)
    a["ctx_v"] = i["cache_na_v"][0].transpose(0, 2, 1, 3).reshape(DEPTH, P, 512)
    rb = i["rel_bias"].reshape(DEPTH * 8, 15 * 31)
    rb = np.concatenate([rb, np.full((DEPTH * 8, 1), -1e30, f), np.zeros((DEPTH * 8, 1), f)], 1)
    where = np.full((P, 3, 384), 15 * 31 + 1)
    for kind, blk in ((0, 0), (1, 1), (2, 3)):
        c, r = np.divmod(np.arange(P), GR)
        c2, r2 = np.divmod(np.arange(256), GR)
        c, c2 = c + 16 * blk, c2 + KEY_START[blk]
        lo = np.clip(c - 8, 0, GW - 16)[:, None]
        inside = (c2[None] >= lo) & (c2[None] < lo + 16)
        at = (r2[None] - r[:, None] + 7) * 31 + c2[None] - c[:, None] + 15
        where[:, kind, :256] = np.where(inside, at, 15 * 31)
    a["bias"] = rb[:, where].reshape(DEPTH, PAIRS, 2, P, 3, 384)
    eye, p = np.eye(P, dtype=f), np.arange(P)
    swap = np.zeros((P, P), f)
    low = p % 16 < 8
    swap[np.where(low, p + 8, p - 8), p] = np.where(low, -1, 1)
    a["mats"] = np.stack([eye, (p[:, None] // 64 == p // 64).astype(f), np.ones((P, P), f), swap], 1)
    tok = np.arange(LAT)
    inv = (f(10000.0) ** (-np.arange(0, 16, 2, dtype=f) / f(16))).astype(f)
    pos = np.where((p % 32 < 16)[:, None], (tok // GW)[None], (tok % GW)[None]).astype(f)
    ang = pos * inv[p % 8][:, None]
    rope = np.zeros((P, 2, T), f)
    rope[:, 0, LAT:] = 1
    rope[:, 0, :LAT], rope[:, 1, :LAT] = np.cos(ang), np.sin(ang)
    a["rope"] = rope
    s = (p % CHUNK)[:, None]
    tt = np.arange(4)[:, None, None] * SUB + np.zeros((1, 4, 1), int) + np.arange(SUB)
    tt = tt.reshape(1, 256)
    a["causal"] = np.concatenate([s <= tt, s >= tt], 1).astype(f)
    a["heads4"] = (p[:, None] // 32 == np.arange(4)).astype(f)
    win = np.array([[2, 4], [8, 16]])[:, p // 64].T
    a["inv_w"] = (1.0 / win).astype(f)
    edges = np.ones((P, 2, 2, 2, 8), f)
    for st, n in enumerate((LAT, CTX)):
        for e, ts in enumerate((np.arange(8), np.arange(n - 8, n))):
            half = win[:, :, None] // 2
            count = np.minimum(ts + half, n) - np.maximum(ts - half, 0)
            edges[:, :, st, e, :] = win[:, :, None] / count
    a["edges"] = edges
    return {n: np.ascontiguousarray(v) for n, v in a.items()}


_OUTS = {"x": (P, KT, T), "k": (DEPTH, PAIRS, P, CTX), "v": (DEPTH, PAIRS, P, CTX), "s": (DEPTH, P, 2, CHUNK)}


def kernel(**inputs):
    import numpy as np
    import concourse.bacc as bacc
    from concourse.bass_utils import run_bass_kernel_spmd

    arrays = layout({n: np.asarray(v) for n, v in inputs.items()})
    nc = bacc.Bacc("TRN2", target_bir_lowering=False, num_devices=1)
    a = {n: nc.dram_tensor(f"in_{n}", v.shape, mybir.dt.from_np(v.dtype), kind="ExternalInput").ap() for n, v in arrays.items()}
    out = {n: nc.dram_tensor(f"out_{n}", s, F32, kind="ExternalOutput").ap() for n, s in _OUTS.items()}
    build(nc, a, out)
    r = run_bass_kernel_spmd(nc, [{f"in_{n}": v for n, v in arrays.items()}], core_ids=[0]).results[0]
    y = r["out_x"].transpose(1, 0, 2).reshape(D, T).T
    k, v = (r[f"out_{n}"].reshape(1, DEPTH, 8, 64, CTX).transpose(0, 1, 2, 4, 3) for n in "kv")
    s = r["out_s"].reshape(1, DEPTH, 4, 32, 2, CHUNK)
    return y[LAT:][None], y[:LAT][None], k, v, s[:, :, :, :, 0], s[:, :, :, :, 1]
```
